# Optimizing a Trainium2 kernel written in Bass

```python
import math
import jax, jax.numpy as jnp
from jax import lax
import numpy as np

D_MODEL = 1024
BATCH = 1
SEQ = 1024
DEPTH = 1

CHUNK = 64
N_META = 16
N_SB_HEADS = 8
SB_HEAD_DIM = 64
SB_WIDTH = N_SB_HEADS * SB_HEAD_DIM
CONV_CHANNELS = 512
CONV_KERNEL = 31
MIX_WIDTH = SB_WIDTH + CONV_CHANNELS
IN_COLS = 3 * SB_WIDTH + 2 * CONV_CHANNELS
D_FF = ((8 * D_MODEL // 3 + 255) // 256) * 256
QUERY_BLOCK = 128
EPS = 1e-6

kernel_name = "hybrid_stickbreak_conformer_conv_block"

def _rmsnorm(x, g):
    xf = x.astype(jnp.float32)
    y = xf * lax.rsqrt(jnp.mean(xf * xf, axis=-1, keepdims=True) + EPS)
    return (y * g.astype(jnp.float32)).astype(x.dtype)

def _layernorm(x, g, b):
    xf = x.astype(jnp.float32)
    mu = jnp.mean(xf, axis=-1, keepdims=True)
    var = jnp.mean(jnp.square(xf - mu), axis=-1, keepdims=True)
    y = (xf - mu) * lax.rsqrt(var + EPS)
    return (y * g.astype(jnp.float32) + b.astype(jnp.float32)).astype(x.dtype)

def _stick_breaking_attention(q, k, v):
    b, l, h, dh = q.shape
    n_blocks = -(-l // QUERY_BLOCK)
    lp = n_blocks * QUERY_BLOCK
    pad = [(0, 0), (0, lp - l), (0, 0), (0, 0)]
    q = jnp.pad(q, pad)
    k = jnp.pad(k, pad)
    v = jnp.pad(v, pad)
    scale = 1.0 / math.sqrt(dh)
    q_blocks = q.reshape(b, n_blocks, QUERY_BLOCK, h, dh).transpose(1, 0, 2, 3, 4)
    starts = jnp.arange(n_blocks, dtype=jnp.int32) * QUERY_BLOCK
    key_pos = jnp.arange(lp, dtype=jnp.int32)

    def one_block(args):
        qi, start = args
        z = jnp.einsum('bqhd,bkhd->bhqk', qi, k).astype(jnp.float32) * scale
        t = start + jnp.arange(QUERY_BLOCK, dtype=jnp.int32)
        mask = key_pos[None, :] < t[:, None]
        log_beta = jax.nn.log_sigmoid(z)
        log_1m_beta = jnp.where(mask, jax.nn.log_sigmoid(-z), 0.0)
        rev = lax.cumsum(log_1m_beta, axis=3, reverse=True)
        excl = jnp.concatenate([rev[..., 1:], jnp.zeros_like(rev[..., :1])], axis=-1)
        w = jnp.where(mask, jnp.exp(log_beta + excl), 0.0)
        return jnp.einsum('bhqk,bkhd->bqhd', w.astype(v.dtype), v)

    out = lax.map(one_block, (q_blocks, starts))
    out = out.transpose(1, 0, 2, 3, 4).reshape(b, lp, h, dh)
    return out[:, :l]

def _conformer_conv(a, gate, dw_w, dw_b, ln_g, ln_b):
    u = a * jax.nn.sigmoid(gate)
    c = u.shape[-1]
    u = lax.conv_general_dilated(
        u, dw_w.astype(u.dtype)[:, None, :], window_strides=(1,),
        padding=[(CONV_KERNEL - 1, 0)],
        dimension_numbers=('NWC', 'WIO', 'NWC'), feature_group_count=c)
    u = u + dw_b.astype(u.dtype)
    u = _layernorm(u, ln_g, ln_b)
    return jax.nn.silu(u)

def setup_inputs(seed: int = 0) -> dict:
    key = jax.random.key(seed)
    ks = jax.random.split(key, 16)
    f32 = jnp.float32
    nrm = lambda k, shape, s: jax.random.normal(k, shape, f32) * s
    return {
        "x": jax.random.normal(ks[0], (BATCH, SEQ, D_MODEL), f32),
        "meta_tokens": nrm(ks[1], (N_META, D_MODEL), 1.0),
        "mix_norm_g": 1.0 + nrm(ks[2], (DEPTH, D_MODEL), 0.02),
        "w_in": nrm(ks[3], (DEPTH, D_MODEL, IN_COLS), D_MODEL ** -0.5),
        "conv_dw_w": nrm(ks[4], (DEPTH, CONV_KERNEL, CONV_CHANNELS), CONV_KERNEL ** -0.5),
        "conv_dw_b": nrm(ks[5], (DEPTH, CONV_CHANNELS), 0.02),
        "conv_ln_g": 1.0 + nrm(ks[6], (DEPTH, CONV_CHANNELS), 0.02),
        "conv_ln_b": nrm(ks[7], (DEPTH, CONV_CHANNELS), 0.02),
        "w_out": nrm(ks[8], (DEPTH, MIX_WIDTH, D_MODEL), MIX_WIDTH ** -0.5),
        "ffn_norm_g": 1.0 + nrm(ks[9], (DEPTH, D_MODEL), 0.02),
        "w_gate": nrm(ks[10], (DEPTH, D_MODEL, D_FF), D_MODEL ** -0.5),
        "w_up": nrm(ks[11], (DEPTH, D_MODEL, D_FF), D_MODEL ** -0.5),
        "w_down": nrm(ks[12], (DEPTH, D_FF, D_MODEL), D_FF ** -0.5),
        "final_norm_g": 1.0 + nrm(ks[13], (D_MODEL,), 0.02),
    }

def reference(x, meta_tokens, mix_norm_g, w_in, conv_dw_w, conv_dw_b, conv_ln_g, conv_ln_b,
              w_out, ffn_norm_g, w_gate, w_up, w_down, final_norm_g):
    b = x.shape[0]
    meta = jnp.broadcast_to(meta_tokens.astype(x.dtype)[None], (b, N_META, D_MODEL))
    h = jnp.concatenate([meta, x], axis=1)
    l = h.shape[1]
    for i in range(DEPTH):
        hn = _rmsnorm(h, mix_norm_g[i])
        proj = jnp.einsum('bld,dc->blc', hn, w_in[i])
        q, k, v, ca, cg = jnp.split(
            proj, [SB_WIDTH, 2 * SB_WIDTH, 3 * SB_WIDTH, 3 * SB_WIDTH + CONV_CHANNELS], axis=-1)
        heads = lambda t: t.reshape(b, l, N_SB_HEADS, SB_HEAD_DIM)
        attn = _stick_breaking_attention(heads(q), heads(k), heads(v)).reshape(b, l, SB_WIDTH)
        conv = _conformer_conv(ca, cg, conv_dw_w[i], conv_dw_b[i], conv_ln_g[i], conv_ln_b[i])
        mixed = jnp.concatenate([attn, conv], axis=-1)
        h = h + jnp.einsum('blc,cd->bld', mixed, w_out[i])
        hn = _rmsnorm(h, ffn_norm_g[i])
        g = jnp.einsum('bld,df->blf', hn, w_gate[i])
        u = jnp.einsum('bld,df->blf', hn, w_up[i])
        h = h + jnp.einsum('blf,fd->bld', jax.nn.silu(g) * u, w_down[i])
    h = _rmsnorm(h, final_norm_g)
    return h[:, N_META:]


_drawn_inputs = setup_inputs


def setup_inputs(seed=0):
    import zlib

    import numpy as np

    out = dict(_drawn_inputs(seed))
    spreads = {}
    factors = {'mix_norm_g': 4.137,
     'conv_dw_b': 3.813,
     'conv_ln_g': 15.863,
     'conv_ln_b': 36.056,
     'ffn_norm_g': 4.37,
     'final_norm_g': 20.543}
    for name, (base, spread) in spreads.items():
        noise = np.random.default_rng([zlib.crc32(name.encode()), seed]).standard_normal(out[name].shape)
        drawn = base * np.exp(spread * noise) if base else spread * noise
        out[name] = __import__('jax').numpy.asarray(drawn.astype(out[name].dtype))
    for name, factor in factors.items():
        out[name] = (out[name] * factor).astype(out[name].dtype)
    return out
```

```python
import math
from contextlib import ExitStack

import concourse.bass as bass
from concourse import mybir

F32 = mybir.dt.float32
F32R = mybir.dt.float32r
BF16 = mybir.dt.bfloat16
ALU = mybir.AluOpType
ACT = mybir.ActivationFunctionType

P = 128
BANK = 512
PASSES = ((0, 0), (0, 1), (1, 0))


def hybrid_block(nc, x, meta_tokens, mix_norm_g, w_in, conv_dw_w, conv_dw_b, conv_ln_g, conv_ln_b,
                 w_out, ffn_norm_g, w_gate, w_up, w_down, final_norm_g, out, v_dram):
    D = x.shape[2]
    L = x.shape[1]
    META = meta_tokens.shape[0]
    T = META + L
    KD = D // P
    TILES = L // P
    CONV_K, CH = conv_dw_w.shape[1], conv_dw_w.shape[2]
    FF = w_gate.shape[2]
    CHUNKS = FF // P // 2
    SB = w_out.shape[1] - CH
    DH = 64
    PAIRS = SB // (2 * DH)
    KB = T // P + 1
    PAD = CONV_K - 1 - META
    SCALE = 1.0 / math.sqrt(DH)
    EPS = 1e-6
    assert PAIRS == CH // P == 4 and TILES == 8 and KD == 8

    w_in_t = w_in[0].rearrange("(k p) c -> p k c", p=P)
    w_out_t = w_out[0].rearrange("(k p) c -> p k c", p=P)
    w_gate_t = w_gate[0].rearrange("(k p) c -> p k c", p=P)
    w_up_t = w_up[0].rearrange("(k p) c -> p k c", p=P)
    w_down_t = w_down[0].rearrange("(f p) c -> p f c", p=P)
    Q0, K0, V0, CA0, CG0 = 0, SB, 2 * SB, 3 * SB, 3 * SB + CH

    W3 = 2 * (-(-T // 6))
    ALL_TOKENS = [(g * W3, min(W3, T - g * W3)) for g in range(3)]
    OUT_TOKENS = [(META + g * BANK, BANK) for g in range(L // BANK)]

    UNITS = [(h, i) for h in range(2) for i in range(TILES)]

    def width(i):
        return META + P * (i + 1)

    def z_chunks(i):
        w = width(i)
        n = -(-w // BANK)
        c = max(2 * (-(-w // (2 * n))), 256)
        return [(a, min(c, max(w - a, 256)), min(c, w - a)) for a in range(0, w, c)]

    def t_banks(i):
        nb = i + 2
        return [range(a, min(a + 4, nb)) for a in range(0, nb, 4)]

    def counted(f):
        c = [0]
        for _, i in UNITS:
            c.append(c[-1] + len(f(i)))
        return c

    CZ, CT = counted(z_chunks), counted(t_banks)
    NZ, NT, NU, NG = CZ[-1], CT[-1], len(UNITS), len(UNITS) // 4
    assert NZ % 2 == 0 and NT % 4 == 0

    GROUPS = ([("k", g) for g in range(3)] + [("q", g) for g in range(2)]
              + [("cg", g) for g in range(3)] + [("ca", g) for g in range(3)])
    FIRST = 5
    DVE_G = {("k", g): g for g in range(3)} | {("q", g): 3 + g for g in range(2)} | {("ca", g): 5 + g for g in range(3)}
    NP = CONV_K + 3

    ctx = ExitStack()
    with ctx:
        def sem(name):
            return ctx.enter_context(nc.semaphore(name))

        def region(name, size, *stages):
            found = []
            for tensors in stages:
                with ExitStack() as stack:
                    for n, shape, dt in tensors:
                        found.append(stack.enter_context(nc.sbuf_tensor(n, shape, dt)))
            ctx.enter_context(nc.sbuf_tensor(name, [P, size], F32))
            return found

        (hn_hi, hn_lo, wo_hi, wo_lo, gu1_hi, gu1_lo, wd_hi, wd_lo, wd_raw, act_hi, act_lo, sil, prod) = region(
            "region1", 2 * KD * T,
            [("hn_hi", [P, KD, T], F32R), ("hn_lo", [P, KD, T], F32R)],
            [("wo_hi", [P, KD, D], F32R), ("wo_lo", [P, KD, D], F32R)],
            [("gu1_hi", [P, 2, KD, P], F32R), ("gu1_lo", [P, 2, KD, P], F32R),
             ("wd_hi", [P, 2, D], F32R), ("wd_lo", [P, 2, D], F32R), ("wd_raw", [P, 2, D], F32),
             ("act_hi", [P, 2, L], F32R), ("act_lo", [P, 2, L], F32R),
             ("sil", [P, L], F32), ("prod", [P, L], F32)])
        (xin, xnorm, g1b, v_stage, qst, kd, wbeta, gq, w_t, vs, hn2_hi, hn2_lo) = region(
            "region2", 2 * KD * L,
            [("xin", [P, 2, D], F32), ("xnorm", [P, 2, D], F32), ("g1b", [P, D], F32),
             ("v_stage", [P, 2, SB], F32)],
            [("qst", [P, 2, L], F32R), ("kd", [P, 2, 2, T], F32R), ("wbeta", [P, 3, KB * P], F32),
             ("gq", [P, 3, T], F32), ("w_t", [P, 4, 4, P], F32), ("vs", [P, KB, P], F32)],
            [("hn2_hi", [P, KD, L], F32R), ("hn2_lo", [P, KD, L], F32R)])
        (wv_hi, wv_lo, mix) = region(
            "region3", KD * L,
            [("wv_hi", [P, KD, SB], F32R), ("wv_lo", [P, KD, SB], F32R)],
            [("mix", [P, TILES, KD, P], F32)])
        (wp_hi, wp_lo, ms_hi, ms_lo, xn2, g2b, ost, gfb) = region(
            "region4", 4 * KD * P,
            [("wp_hi", [P, 2, KD, P], F32R), ("wp_lo", [P, 2, KD, P], F32R)],
            [("ms_hi", [P, 2, 4, P], F32R), ("ms_lo", [P, 2, 4, P], F32R), ("xn2", [P, D], F32),
             ("g2b", [P, D], F32)],
            [("ost", [P, 2, D], F32), ("gfb", [P, D], F32)])
        (par_nat, u_pad, u_next, acc, gu0_hi, gu0_lo) = region(
            "region5", PAD + 2 * T + 2 * L,
            [("par_nat", [NP, CH], F32)],
            [("u_pad", [P, PAD + T], F32), ("u_next", [P, T], F32), ("acc", [P, 2, L], F32)],
            [("gu0_hi", [P, 2, KD, P], F32R), ("gu0_lo", [P, 2, KD, P], F32R)])

        def keep(name, shape, dt):
            return ctx.enter_context(nc.sbuf_tensor(name, shape, dt))

        raw = keep("raw", [P, 2, KD * P], F32)
        ones = keep("ones", [P, 1], F32)
        zeros = keep("zeros", [P, 1], F32)
        ident = keep("ident", [P, P], F32)
        ident_bf = keep("ident_bf", [P, P], BF16)
        mask_bf = keep("mask_bf", [P, P], BF16)
        par = keep("par", [P, 4, NP], F32)
        parp = keep("parp", [P, NP], F32)
        half = keep("half", [P, 1], F32)
        sumsq = keep("sumsq", [P, 3 * (TILES + 1)], F32)
        var = keep("var", [P, 3 * (TILES + 1)], F32)
        rstd = keep("rstd", [P, 3 * (TILES + 1)], F32)
        bn6 = keep("bn6", [P, 6], F32)
        bn2 = keep("bn2", [P, 2 * TILES], F32)
        ln_var = keep("ln_var", [P, TILES], F32)
        ln_rstd = keep("ln_rstd", [P, TILES], F32)

        ps = ctx.enter_context(nc.psum_tensor("ps", [P, 8, BANK], F32))
        PJ, Z, TB, PV = 0, 2, 4, 6

        gu_hi, gu_lo = [gu0_hi, gu1_hi], [gu0_lo, gu1_lo]

        par_loaded, g1_loaded, g2_loaded, gf_loaded = sem("par_loaded"), sem("g1_loaded"), sem("g2_loaded"), sem("gf_loaded")
        x_loaded = [sem("x_loaded0"), sem("x_loaded1")]
        consts, par_t, par_ready = sem("consts"), sem("par_t"), sem("par_ready")
        x_sumsq, x_var, x_rstd, xn_ready = sem("x_sumsq"), sem("x_var"), sem("x_rstd"), sem("xn_ready")
        xt_ready, xhi_ready, xlo_ready = sem("xt_ready"), sem("xhi_ready"), sem("xlo_ready")
        raw_loaded = [sem("raw_loaded0"), sem("raw_loaded1")]
        whi_done, wlo_done = sem("whi_done"), sem("wlo_done")
        v_ready, v_copied = sem("v_ready"), sem("v_copied")
        v_stored = [sem("v_stored0"), sem("v_stored1")]
        pj_ready, pj_free_dve, pj_free_act = sem("pj_ready"), sem("pj_free_dve"), sem("pj_free_act")
        pj_hi = sem("pj_hi")
        k_dup, v_loaded, v_zeroed = sem("k_dup"), sem("v_loaded"), sem("v_zeroed")
        u_zeroed, u_ready, conv_step = sem("u_zeroed"), sem("u_ready"), sem("conv_step")
        z_ready, z_free, scanned, w_ready = sem("z_ready"), sem("z_free"), sem("scanned"), sem("w_ready")
        tail_zeroed, t_ready, t_copied, pv_used, pv_evac = sem("tail_zeroed"), sem("t_ready"), sem("t_copied"), sem("pv_used"), sem("pv_evac")
        ln_t, ln_stat, ln_agg, ln_var_s, ln_rstd_s, ln_norm = sem("ln_t"), sem("ln_stat"), sem("ln_agg"), sem("ln_var_s"), sem("ln_rstd_s"), sem("ln_norm")
        ln_back, ln_silu, ms_hi_s, ms_lo_s, ms_used = sem("ln_back"), sem("ln_silu"), sem("ms_hi_s"), sem("ms_lo_s"), sem("ms_used")
        wo_ready, h_ready = sem("wo_ready"), sem("h_ready")
        xres_loaded = [sem("xres_loaded0"), sem("xres_loaded1")]
        h_sumsq, h_var, h_rstd, hn_ready = sem("h_sumsq"), sem("h_var"), sem("h_rstd"), sem("hn_ready")
        ht_ready, hhi_ready, hlo_ready = sem("ht_ready"), sem("hhi_ready"), sem("hlo_ready")
        wd_loaded, dhi_done, dlo_done = sem("wd_loaded"), sem("dhi_done"), sem("dlo_done")
        g_ready, u_ready2, silu_done, prod_done = sem("g_ready"), sem("u_ready2"), sem("silu_done"), sem("prod_done")
        act_hi_s, act_lo_s, d_ready, d_added = sem("act_hi_s"), sem("act_lo_s"), sem("d_ready"), sem("d_added")
        o_sumsq, o_var, o_rstd, o_ready = sem("o_sumsq"), sem("o_var"), sem("o_rstd"), sem("o_ready")
        o_stored = [sem("o_stored0"), sem("o_stored1")]

        block = ctx.enter_context(nc.Block())

        CH_V, CH_CG0, CH_CA0, CH_K0, CH_Q0 = 0, 4, 5, 6, 7
        CH_LOOP = 8
        CH_WO = CH_LOOP + 4 * (PAIRS - 1)
        CH_GU = CH_WO + KD

        def pj_bank(kind, g):
            return PJ + GROUPS.index((kind, g)) % 2

        def pj_count(kind, g, p):
            return 6 + 11 * p + GROUPS.index((kind, g)) + 1

        def used_up(kind, p):
            return pj_ready, pj_count(kind, 1 if kind == "q" else 2, p)

        def freed(kind, g, p):
            if kind == "cg":
                return pj_free_act, 3 + 3 * p + g + 1
            return pj_free_dve, 3 + 8 * p + DVE_G[kind, g] + 1

        def tok(kind, g):
            return OUT_TOKENS[g] if kind == "q" else ALL_TOKENS[g]

        def chunk_loaded(j):
            return raw_loaded[j % 2], 16 * (j // 2 + 1)

        @block.sync
        def _(sp):
            sp.dma_start(par_nat[0:CONV_K, :], conv_dw_w[0]).then_inc(par_loaded, 16)
            for n, v in enumerate((conv_dw_b, conv_ln_g, conv_ln_b)):
                sp.dma_start(par_nat[CONV_K + n:CONV_K + n + 1, :], v[0:1, :]).then_inc(par_loaded, 16)
            sp.dma_start(g1b[:, :], mix_norm_g[0].partition_broadcast(P)).then_inc(g1_loaded, 16)

            def load_x(t):
                if t >= 2:
                    sp.wait_ge(xn_ready, t - 1)
                if t == 0:
                    sp.dma_start(xin[0:META, 0, :], meta_tokens).then_inc(x_loaded[0], 16)
                else:
                    sp.dma_start(xin[:, t % 2, :], x[0, (t - 1) * P:t * P, :]).then_inc(x_loaded[t % 2], 16)

            def load_chunk(j, dst, src, slot=None):
                sp.wait_ge(wlo_done, j - 1)
                sp.dma_start(dst, src).then_inc(raw_loaded[slot], 16)

            def tile_of(slot):
                return raw[:, slot, :].rearrange("p (k c) -> p k c", k=KD)

            def load_tile(j, slot, src_t, col):
                load_chunk(j, tile_of(slot), src_t[:, :, bass.ds(col, P)], slot)

            load_x(0)
            load_x(1)
            for j in range(4):
                if j < 2:
                    sp.dma_start(raw[:, j, :].rearrange("p (k c) -> p k c", k=2),
                                 w_in_t[:, 2 * j:2 * j + 2, V0:V0 + SB]).then_inc(raw_loaded[j], 16)
                else:
                    load_chunk(j, raw[:, j % 2, :].rearrange("p (k c) -> p k c", k=2),
                               w_in_t[:, 2 * j:2 * j + 2, V0:V0 + SB], j % 2)
                load_x(2 + j)
            for t in range(6, TILES + 1):
                load_x(t)
            load_tile(CH_CG0, 0, w_in_t, CG0)
            load_tile(CH_CA0, 1, w_in_t, CA0)
            load_tile(CH_K0, 0, w_in_t, K0)
            load_tile(CH_Q0, 1, w_in_t, Q0)
            sp.wait_ge(v_stored[0], 16 * 5)
            sp.wait_ge(v_stored[1], 16 * 4)
            sp.wait_ge(v_zeroed, 1)

            def pair_loads(p, more):
                if more:
                    load_tile(CH_LOOP + 4 * p, 0, w_in_t, CG0 + P * (p + 1))
                    load_tile(CH_LOOP + 4 * p + 1, 1, w_in_t, CA0 + P * (p + 1))
                else:
                    for k in range(2):
                        load_chunk(CH_WO + k, raw[:, k, :], w_out_t[:, k, :], k)
                sp.wait_ge(pv_used, NT * p)
                FB = T // P
                sp.dma_start(vs[:, 0:FB, :], v_dram[0:FB * P, bass.ds(P * p, P)].rearrange(
                    "(b p) c -> p b c", p=P)).then_inc(v_loaded, 16)
                sp.dma_start(vs[0:T - FB * P, FB, :], v_dram[FB * P:T, bass.ds(P * p, P)]).then_inc(v_loaded, 16)
                sp.wait_ge(pj_free_dve, 3 + 8 * p + 3)
                sp.dma_start(kd[DH:2 * DH, :, :, :].bitcast(F32), kd[0:DH, :, :, :].bitcast(F32)).then_inc(k_dup, 16)
                if more:
                    load_tile(CH_LOOP + 4 * p + 2, 0, w_in_t, K0 + P * (p + 1))
                    load_tile(CH_LOOP + 4 * p + 3, 1, w_in_t[:, :, Q0 + P:Q0 + SB], P * p)

            with sp.Fori(0, PAIRS - 1) as p:
                pair_loads(p, True)
            pair_loads(PAIRS - 1, False)
            for k in range(2, KD):
                load_chunk(CH_WO + k, raw[:, k % 2, :], w_out_t[:, k, :], k % 2)
            sp.wait_ge(*used_up("q", PAIRS - 1))
            sp.dma_start(g2b[:, :], ffn_norm_g[0].partition_broadcast(P)).then_inc(g2_loaded, 16)
            load_tile(CH_GU, 0, w_gate_t, 0)
            load_tile(CH_GU + 1, 1, w_up_t, 0)
            for i in range(TILES):
                sp.wait_ge(ms_lo_s, 2 * i + 2)
                sp.dma_start(mix[:, i, :, :].rearrange("p k t -> p (k t)"),
                             x[0, i * P:(i + 1) * P, :]).then_inc(xres_loaded[i % 2], 16)
            sp.wait_ge(wo_ready, 2 * TILES)
            sp.wait_ge(ht_ready, TILES)
            sp.dma_start(gfb[:, :], final_norm_g.partition_broadcast(P)).then_inc(gf_loaded, 16)

            def ffn_loads(c, more):
                f = 2 * c
                load_tile(CH_GU + 2 * f + 2, 0, w_gate_t, P * (f + 1))
                load_tile(CH_GU + 2 * f + 3, 1, w_up_t, P * (f + 1))
                sp.wait_ge(dlo_done, c)
                sp.dma_start(wd_raw[:, :, :], w_down_t[:, bass.ds(f, 2), :]).then_inc(wd_loaded, 16)
                if more:
                    load_tile(CH_GU + 2 * f + 4, 0, w_gate_t, P * (f + 2))
                    load_tile(CH_GU + 2 * f + 5, 1, w_up_t, P * (f + 2))

            with sp.Fori(0, CHUNKS - 1) as c:
                ffn_loads(c, True)
            ffn_loads(CHUNKS - 1, False)
            for i in range(TILES):
                sp.wait_ge(o_ready, i + 1)
                sp.dma_start(out[0, i * P:(i + 1) * P, :], ost[:, i % 2, :]).then_inc(o_stored[i % 2], 16)
            for s in o_stored:
                sp.wait_ge(s, 16 * TILES // 2)

        @block.gpsimd
        def _(pool):
            pool.memset(ident[:, :], 0.0).then_inc(consts, 1)
            pool.memset(ident_bf[:, :], 0.0).then_inc(consts, 1)
            pool.memset(mask_bf[:, :], -1e30).then_inc(consts, 1)
            pool.memset(half[:, :], -0.5).then_inc(consts, 1)
            pool.memset(ones[:, :], 1.0).then_inc(consts, 1)
            pool.memset(zeros[:, :], 0.0).then_inc(consts, 1)
            pool.wait_ge(consts, 6)
            pool.affine_select(out=ident[:, :], in_=ident[:, :], compare_op=ALU.not_equal, fill=1.0,
                               base=0, pattern=[[-1, P]], channel_multiplier=1).then_inc(consts, 1)
            pool.affine_select(out=ident_bf[:, :], in_=ident_bf[:, :], compare_op=ALU.not_equal, fill=1.0,
                               base=0, pattern=[[-1, P]], channel_multiplier=1).then_inc(consts, 1)
            pool.affine_select(out=mask_bf[:, :], in_=mask_bf[:, :], compare_op=ALU.is_ge, fill=0.0,
                               base=0, pattern=[[1, P]], channel_multiplier=-1).then_inc(consts, 1)

            def root(src, v, dst, scale, ready, n, v_sem, r_sem):
                pool.wait_ge(ready, n)
                pool.tensor_scalar(v, src, scale, EPS, ALU.mult, ALU.add).then_inc(v_sem, 1)
                pool.wait_ge(v_sem, n)
                rows = src.shape[0]
                pool.tensor_tensor(dst, v, half[0:rows, :], ALU.pow).then_inc(r_sem, 1)

            def x_root(t):
                r = META if t == 0 else P
                root(sumsq[0:r, t:t + 1], var[0:r, t:t + 1], rstd[0:r, t:t + 1], 1.0 / D, x_sumsq, t + 1, x_var, x_rstd)

            def lo(j, slot, dst, hi):
                pool.wait_ge(whi_done, j + 1)
                pool.tensor_tensor(dst, raw[:, slot, :], hi.bitcast(F32), ALU.subtract).then_inc(wlo_done, 1)

            def wp(t, slot):
                return t[:, slot, :, :].rearrange("p k c -> p (k c)")

            def wv(t, j):
                return t[:, 2 * j:2 * j + 2, :].rearrange("p k c -> p (k c)")

            x_root(0)
            x_root(1)
            for t in range(2, TILES + 1):
                if t < 6:
                    lo(t - 2, t % 2, wv(wv_lo, t - 2), wv(wv_hi, t - 2))
                x_root(t)
            for j in (CH_CG0, CH_CA0, CH_K0, CH_Q0):
                lo(j, j % 2, wp(wp_lo, j % 2), wp(wp_hi, j % 2))
            pool.wait_ge(par_ready, 1)
            pool.memset(u_pad[:, 0:PAD], 0.0).then_inc(u_zeroed, 1)
            pool.wait_ge(xlo_ready, TILES + 1)
            pool.wait_ge(v_stored[0], 16 * 5)
            pool.wait_ge(v_stored[1], 16 * 4)
            pool.memset(vs[:, KB - 1, :], 0.0).then_inc(v_zeroed, 1)

            def pair(p, more):
                if more:
                    for n in range(2):
                        lo(CH_LOOP + 4 * p + n, n, wp(wp_lo, n), wp(wp_hi, n))
                for n, (h, i) in enumerate(UNITS):
                    if i < 3:
                        pool.wait_ge(t_ready, NT * p + (CT[n - 2] if n >= 3 else 0))
                        zero = zeros[:, :].broadcast_to([P, KB * P - width(i)])
                        pool.tensor_tensor(wbeta[:, n % 3, width(i):KB * P], zero, zero, ALU.mult).then_inc(tail_zeroed, 1)
                    if i == 2 and h == 0 and more:
                        for m in (2, 3):
                            lo(CH_LOOP + 4 * p + m, m % 2, wp(wp_lo, m % 2), wp(wp_hi, m % 2))

            with pool.Fori(0, PAIRS - 1) as p:
                pair(p, True)
            pair(PAIRS - 1, False)
            for k in range(KD):
                lo(CH_WO + k, k % 2, wo_lo[:, k, :], wo_hi[:, k, :])
            for n in range(2):
                lo(CH_GU + n, n, wp(gu0_lo, n), wp(gu0_hi, n))
            for i in range(TILES):
                pool.wait_ge(ln_agg, i + 1)
                pool.tensor_scalar(ln_var[:, i:i + 1], bn2[:, 2 * i + 1:2 * i + 2], 1.0, EPS, ALU.mult, ALU.add).then_inc(ln_var_s, 1)
                pool.wait_ge(ln_var_s, i + 1)
                pool.tensor_tensor(ln_rstd[:, i:i + 1], ln_var[:, i:i + 1], half[:, :], ALU.pow).then_inc(ln_rstd_s, 1)
                if i >= 1:
                    h_root = TILES + i
                    root(sumsq[:, h_root:h_root + 1], var[:, h_root:h_root + 1], rstd[:, h_root:h_root + 1],
                         1.0 / D, h_sumsq, i, h_var, h_rstd)
            n = 2 * TILES
            root(sumsq[:, n:n + 1], var[:, n:n + 1], rstd[:, n:n + 1], 1.0 / D, h_sumsq, TILES, h_var, h_rstd)

            def ffn(c, more):
                f = 2 * c
                for n in range(2):
                    lo(CH_GU + 2 * f + 2 + n, n, wp(gu1_lo, n), wp(gu1_hi, n))
                if more:
                    for n in range(2):
                        lo(CH_GU + 2 * f + 4 + n, n, wp(gu0_lo, n), wp(gu0_hi, n))
                pool.wait_ge(dhi_done, c + 1)
                pool.tensor_tensor(wd_lo[:, :, :], wd_raw[:, :, :], wd_hi[:, :, :].bitcast(F32), ALU.subtract).then_inc(dlo_done, 1)

            with pool.Fori(0, CHUNKS - 1) as c:
                ffn(c, True)
            ffn(CHUNKS - 1, False)
            for i in range(TILES):
                n = 2 * TILES + 1 + i
                root(sumsq[:, n:n + 1], var[:, n:n + 1], rstd[:, n:n + 1], 1.0 / D, o_sumsq, i + 1, o_var, o_rstd)

        @block.scalar
        def _(act):
            def hi(j, slot, dst, wait=None):
                if wait:
                    act.wait_ge(*wait)
                act.wait_ge(raw_loaded[slot], 8 * (j - slot) + 16)
                act.activation(dst, raw[:, slot, :], ACT.Copy).then_inc(whi_done, 1)

            def wp(slot):
                return wp_hi[:, slot, :, :].rearrange("p k c -> p (k c)")

            def square_x(t):
                r = META if t == 0 else P
                act.wait_ge(x_loaded[t % 2], 16 * (t // 2 + 1))
                if t >= 2:
                    act.wait_ge(xt_ready, t - 1)
                act.activation(xnorm[0:r, t % 2, :], xin[0:r, t % 2, :], ACT.Square,
                               accum_out=sumsq[0:r, t:t + 1]).then_inc(x_sumsq, 1)

            def evac_x(t):
                n, c0 = (META, 0) if t == 0 else (P, META + (t - 1) * P)
                act.wait_ge(xt_ready, t + 1)
                b = (TB, Z)[t % 2]
                act.activation(hn_hi[:, :, c0:c0 + n],
                               ps[:, b:b + 2, :].rearrange("p b (k n) -> p (b k) n", k=4)[:, :, 0:n],
                               ACT.Copy).then_inc(xhi_ready, 1)

            def copy_v(b):
                act.wait_ge(v_ready, b + 1)
                if b >= 2:
                    act.wait_ge(v_stored[b % 2], 16 * (b // 2))
                act.activation(v_stage[:, b % 2, :], ps[:, PV + b % 2, :], ACT.Copy).then_inc(v_copied, 1)
                act.wait_ge(v_copied, b + 1)
                if b < T // P:
                    act.dma_start(v_dram[b * P:(b + 1) * P, :], v_stage[:, b % 2, :]).then_inc(v_stored[b % 2], 16)
                else:
                    n = T - b * P
                    act.dma_start(v_dram[b * P:T, :], v_stage[P - n:P, b % 2, :]).then_inc(v_stored[b % 2], 16)

            square_x(0)
            square_x(1)
            for t in range(TILES + 1):
                if t < 4:
                    j = t
                    hi(j, j % 2, wv_hi[:, 2 * j:2 * j + 2, :].rearrange("p k c -> p (k c)"))
                evac_x(t)
                if t + 2 <= TILES:
                    square_x(t + 2)
                if t == 7:
                    hi(CH_CG0, 0, wp(0))
                if t == 8:
                    hi(CH_CA0, 1, wp(1))
                if t >= 3:
                    copy_v(t - 3)
            for b in range(TILES - 2, TILES + 1):
                copy_v(b)

            def sigmoid_gate(p):
                for g, (c0, n) in enumerate(ALL_TOKENS):
                    act.wait_ge(pj_ready, pj_count("cg", g, p))
                    act.activation(u_next[:, c0:c0 + n], ps[:, pj_bank("cg", g), 0:n], ACT.Sigmoid).then_inc(pj_free_act, 1)

            act.wait_ge(par_ready, 1)
            sigmoid_gate(-1)
            hi(CH_K0, 0, wp(0), used_up("cg", -1))
            hi(CH_Q0, 1, wp(1), used_up("ca", -1))
            act.wait_ge(v_stored[0], 16 * 5)
            act.wait_ge(v_stored[1], 16 * 4)
            act.wait_ge(xlo_ready, TILES + 1)

            def split_hi(kind, g, p):
                c0, n = tok(kind, g)
                act.wait_ge(pj_ready, pj_count(kind, g, p))
                if g == 0:
                    act.wait_ge(z_ready, NZ * p)
                for h in range(2):
                    dst = kd[0:DH, h, 0, c0:c0 + n] if kind == "k" else qst[0:DH, h, g * BANK:(g + 1) * BANK]
                    act.activation(dst, ps[DH * h:DH * h + DH, pj_bank(kind, g), 0:n], ACT.Copy).then_inc(pj_hi, 1)

            def pair(p, more):
                act.wait_ge(conv_step, (CONV_K + 1) * p)
                act.wait_ge(pj_free_dve, 3 + 8 * p)
                act.wait_ge(u_zeroed, 1)
                act.activation(parp[:, :], par[:, bass.ds(p, 1), :].rearrange("p a c -> p (a c)"), ACT.Copy).then_inc(u_ready, 1)
                act.activation(u_pad[:, PAD:PAD + T], u_next[:, :], ACT.Copy).then_inc(u_ready, 1)
                for g in range(3):
                    split_hi("k", g, p)
                if more:
                    hi(CH_LOOP + 4 * p, 0, wp(0), used_up("k", p))
                for g in range(2):
                    split_hi("q", g, p)
                if more:
                    hi(CH_LOOP + 4 * p + 1, 1, wp(1), used_up("q", p))
                    act.wait_ge(u_ready, 2 * p + 2)
                    sigmoid_gate(p)
                    hi(CH_LOOP + 4 * p + 2, 0, wp(0), used_up("cg", p))

                def sigmoids(n):
                    h, i = UNITS[n]
                    act.wait_ge(t_ready, NT * p + (CT[n - 2] if n >= 3 else 0))
                    chunks = z_chunks(i)
                    for c, (c0, _, used) in enumerate(chunks):
                        m = CZ[n] + c
                        act.wait_ge(z_ready, NZ * p + m + 1)
                        zp = ps[:, Z + m % 2, 0:used]
                        act.activation(gq[:, n % 3, c0:c0 + used], zp, ACT.Sigmoid, scale=-SCALE)
                        act.activation(wbeta[:, n % 3, c0:c0 + used], zp, ACT.Sigmoid, scale=SCALE).then_inc(z_free, 1)

                def copy_t(n):
                    for b, blocks in enumerate(t_banks(UNITS[n][1])):
                        m = CT[n] + b
                        act.wait_ge(t_ready, NT * p + m + 1)
                        act.wait_ge(pv_used, NT * p + max(m - 3, 0))
                        c = len(blocks) * P
                        act.activation(w_t[:, m % 4, 0:len(blocks), :].rearrange("p b t -> p (b t)"),
                                       ps[:, TB + m % 2, 0:c], ACT.Copy).then_inc(t_copied, 1)

                def evac_attention(g):
                    h = g // 2
                    act.wait_ge(pv_used, NT * p + CT[4 * g + 4])
                    act.activation(mix[DH * h:DH * h + DH, 4 * (g % 2):4 * (g % 2) + 4, bass.ds(p, 1), :].rearrange("p i a t -> p i (a t)"),
                                   ps[DH * h:DH * h + DH, PV + g % 2, :].rearrange("p (i t) -> p i t", i=4),
                                   ACT.Copy).then_inc(pv_evac, 1)

                sigmoids(0)
                sigmoids(1)
                if more:
                    hi(CH_LOOP + 4 * p + 3, 1, wp(1), used_up("ca", p))
                for n in range(NU):
                    if n + 2 < NU:
                        sigmoids(n + 2)
                    copy_t(n)
                    if n % 4 == 0 and n:
                        evac_attention(n // 4 - 1)
                    if not more and n >= NU - KD:
                        k = n - (NU - KD)
                        hi(CH_WO + k, k % 2, wo_hi[:, k, :], used_up("q", p))
                evac_attention(NG - 1)

            with act.Fori(0, PAIRS - 1) as p:
                pair(p, True)
            pair(PAIRS - 1, False)

            act.wait_ge(conv_step, (CONV_K + 1) * PAIRS)
            for n in range(2):
                hi(CH_GU + n, n, gu0_hi[:, n, :, :].rearrange("p k c -> p (k c)"))

            def ln_silu_of(i):
                act.wait_ge(ln_back, i + 1)
                for c in range(4):
                    act.activation(mix[:, i, 4 + c, :], ps[:, Z + 1, c * P:(c + 1) * P], ACT.Silu,
                                   bias=par[:, c, CONV_K + 2:CONV_K + 3],
                                   scale=par[:, c, CONV_K + 1:CONV_K + 2]).then_inc(ln_silu, 1)

            def mix_hi(i, part):
                if i and part == 0:
                    act.wait_ge(ms_used, i)
                if i and part == 1:
                    act.wait_ge(wo_ready, 2 * i)
                if part:
                    act.wait_ge(ln_silu, 4 * (i + 1))
                act.activation(ms_hi[:, part, :, :], mix[:, i, 4 * part:4 * part + 4, :], ACT.Copy).then_inc(ms_hi_s, 1)

            def square_h(i):
                act.wait_ge(h_ready, 2 * (i + 1))
                if i:
                    act.wait_ge(ht_ready, i)
                act.activation(xn2[:, :], mix[:, i, :, :].rearrange("p k t -> p (k t)"), ACT.Square,
                               accum_out=sumsq[:, TILES + 1 + i:TILES + 2 + i]).then_inc(h_sumsq, 1)

            def evac_h(i):
                act.wait_ge(ht_ready, i + 1)
                act.activation(hn2_hi[:, :, i * P:(i + 1) * P],
                               ps[:, TB:TB + 2, :].rearrange("p b (k t) -> p (b k) t", k=4), ACT.Copy).then_inc(hhi_ready, 1)

            act.wait_ge(pv_evac, NG * PAIRS)
            mix_hi(0, 0)
            ln_silu_of(0)
            mix_hi(0, 1)
            for i in range(TILES):
                if i + 1 < TILES:
                    mix_hi(i + 1, 0)
                    ln_silu_of(i + 1)
                if i >= 1:
                    evac_h(i - 1)
                if i + 1 < TILES:
                    mix_hi(i + 1, 1)
                square_h(i)
            evac_h(TILES - 1)

            act.wait_ge(wo_ready, 2 * TILES)

            def ffn_hi(j, n, dst, wait):
                hi(j, n, dst[:, n, :, :].rearrange("p k c -> p (k c)"), wait)

            def silu(f):
                for tg in range(2):
                    act.wait_ge(g_ready, 2 * f + tg + 1)
                    act.wait_ge(prod_done, 2 * f)
                    act.activation(sil[:, tg * BANK:(tg + 1) * BANK], ps[:, PJ + tg, :], ACT.Silu).then_inc(silu_done, 1)

            def act_split(f, slot, before):
                act.wait_ge(d_ready, before)
                act.wait_ge(prod_done, 2 * f + 2)
                act.activation(act_hi[:, slot, :], prod[:, :], ACT.Copy).then_inc(act_hi_s, 1)

            def ffn(c, first, more):
                f = 2 * c
                for n in range(2):
                    ffn_hi(CH_GU + 2 * f + 2 + n, n, gu1_hi, None if first else (u_ready2, 2 * f))
                silu(f)
                if more:
                    for n in range(2):
                        ffn_hi(CH_GU + 2 * f + 4 + n, n, gu0_hi, (u_ready2, 2 * f + 2))
                act_split(f, 0, 16 * c)
                act.wait_ge(wd_loaded, 16 * (c + 1))
                act.activation(wd_hi[:, :, :], wd_raw[:, :, :], ACT.Copy).then_inc(dhi_done, 1)
                silu(f + 1)
                act_split(f + 1, 1, 16 * c)

            ffn(0, True, True)
            with act.Fori(1, CHUNKS - 1) as c:
                ffn(c, False, True)
            ffn(CHUNKS - 1, False, False)
            for i in range(TILES):
                act.wait_ge(d_added, 16 * (CHUNKS - 1) + 2 * (i + 1))
                if i == 0:
                    act.wait_ge(hlo_ready, TILES)
                if i >= 2:
                    act.wait_ge(o_stored[i % 2], 16 * (i // 2))
                act.activation(ost[:, i % 2, :], mix[:, i, :, :].rearrange("p k t -> p (k t)"), ACT.Square,
                               accum_out=sumsq[:, 2 * TILES + 1 + i:2 * TILES + 2 + i]).then_inc(o_sumsq, 1)

        @block.vector
        def _(dve):
            dve.wait_ge(consts, 6)
            dve.wait_ge(par_t, 1)
            dve.tensor_copy(par[:, :, :], ps[:, PJ, 0:4 * NP].rearrange("p (c n) -> p c n", c=4)).then_inc(par_ready, 1)

            def norm_x(t):
                r = META if t == 0 else P
                if t == 0:
                    dve.wait_ge(g1_loaded, 16)
                dve.wait_ge(x_rstd, t + 1)
                dve.scalar_tensor_tensor(out=xnorm[0:r, t % 2, :], in0=xin[0:r, t % 2, :], scalar=rstd[0:r, t:t + 1],
                                         in1=g1b[0:r, :], op0=ALU.mult, op1=ALU.mult).then_inc(xn_ready, 1)

            def lo_x(t):
                n, c0 = (META, 0) if t == 0 else (P, META + (t - 1) * P)
                b = (TB, Z)[t % 2]
                dve.wait_ge(xhi_ready, t + 1)
                dve.tensor_tensor(hn_lo[:, :, c0:c0 + n],
                                  ps[:, b:b + 2, :].rearrange("p b (k n) -> p (b k) n", k=4)[:, :, 0:n],
                                  hn_hi[:, :, c0:c0 + n].bitcast(F32), ALU.subtract).then_inc(xlo_ready, 1)

            norm_x(0)
            norm_x(1)
            for t in range(TILES + 1):
                lo_x(t)
                if t + 2 <= TILES:
                    norm_x(t + 2)

            def glu(g, p):
                c0, n = ALL_TOKENS[g]
                dve.wait_ge(pj_ready, pj_count("ca", g, p))
                dve.wait_ge(pj_free_act, 3 + 3 * p + 3)
                dve.tensor_tensor(u_next[:, c0:c0 + n], ps[:, pj_bank("ca", g), 0:n], u_next[:, c0:c0 + n],
                                  ALU.mult).then_inc(pj_free_dve, 1)

            def split_lo(kind, g, p):
                c0, n = tok(kind, g)
                order = DVE_G[kind, g]
                for h in range(2):
                    dve.wait_ge(pj_hi, 10 * p + 2 * order + h + 1)
                    src = ps[DH * h:DH * h + DH, pj_bank(kind, g), 0:n]
                    if kind == "k":
                        dst, high = kd[0:DH, h, 1, c0:c0 + n], kd[0:DH, h, 0, c0:c0 + n]
                    else:
                        dst, high = qst[DH:2 * DH, h, g * BANK:(g + 1) * BANK], qst[0:DH, h, g * BANK:(g + 1) * BANK]
                    last = dve.tensor_tensor(dst, src, high.bitcast(F32), ALU.subtract)
                last.then_inc(pj_free_dve, 1)

            for g in range(3):
                glu(g, -1)

            def pair(p, more):
                def tap(j):
                    base = (CONV_K + 1) * p
                    if j == 0:
                        dve.wait_ge(u_ready, 2 * p + 2)
                        dve.tensor_scalar(acc[:, 0, :], u_pad[:, 0:L], parp[:, 0:1], parp[:, CONV_K:CONV_K + 1],
                                          ALU.mult, ALU.add).then_inc(conv_step, 1)
                    elif j == 1:
                        dve.tensor_scalar(acc[:, 1, :], u_pad[:, 1:1 + L], parp[:, 1:2], None, ALU.mult).then_inc(conv_step, 1)
                    elif j < CONV_K:
                        dve.wait_ge(conv_step, base + j - 1)
                        dve.scalar_tensor_tensor(out=acc[:, j % 2, :], in0=u_pad[:, j:j + L], scalar=parp[:, j:j + 1],
                                                 in1=acc[:, j % 2, :], op0=ALU.mult, op1=ALU.add).then_inc(conv_step, 1)
                    else:
                        dve.wait_ge(conv_step, base + CONV_K)
                        dve.tensor_tensor(mix[:, :, bass.ds(4 + p, 1), :].rearrange("p i a t -> p i (a t)"),
                                          acc[:, 0, :].rearrange("p (i t) -> p i t", i=TILES),
                                          acc[:, 1, :].rearrange("p (i t) -> p i t", i=TILES), ALU.add).then_inc(conv_step, 1)

                taps = iter(range(CONV_K + 1))

                def some_taps(n):
                    for _ in range(n):
                        j = next(taps, None)
                        if j is not None:
                            tap(j)

                for kind, g in GROUPS if more else GROUPS[:FIRST]:
                    some_taps(3)
                    if kind in "kq":
                        split_lo(kind, g, p)
                    elif kind == "ca":
                        glu(g, p)
                for n, (h, i) in enumerate(UNITS):
                    w = width(i)
                    if not more:
                        some_taps(2)
                    dve.wait_ge(z_free, NZ * p + CZ[n + 1])
                    dve.tensor_tensor_scan(out=gq[:, n % 3, 0:w][:, ::-1],
                                           data0=gq[:, n % 3, 0:w][:, ::-1], data1=ones_row(w),
                                           initial=1.0, op0=ALU.mult, op1=ALU.mult).then_inc(scanned, 1)
                    dve.wait_ge(scanned, NU * p + n + 1)
                    dve.tensor_tensor(wbeta[:, n % 3, 0:w - 1], wbeta[:, n % 3, 0:w - 1], gq[:, n % 3, 1:w],
                                      ALU.mult).then_inc(w_ready, 1)
                some_taps(CONV_K)

            def ones_row(w):
                return ones[:, 0:1].broadcast_to([P, w])

            with dve.Fori(0, PAIRS - 1) as p:
                pair(p, True)
            pair(PAIRS - 1, False)

            def ln_stats(i):
                dve.wait_ge(ln_t, i + 1)
                dve.bn_stats(bn6[:, :], ps[:, Z, :]).then_inc(ln_stat, 1)
                dve.wait_ge(ln_stat, i + 1)
                dve.bn_aggr(bn2[:, 2 * i:2 * i + 2], bn6[:, :]).then_inc(ln_agg, 1)

            def ln_normalise(i):
                dve.wait_ge(ln_rstd_s, i + 1)
                dve.wait_ge(ln_agg, i + 1)
                dve.tensor_scalar(mix[:, i, 4:8, :].rearrange("p k t -> p (k t)"), ps[:, Z, :],
                                  bn2[:, 2 * i:2 * i + 1], ln_rstd[:, i:i + 1], ALU.subtract, ALU.mult).then_inc(ln_norm, 1)

            def mix_lo(i, part):
                dve.wait_ge(ms_hi_s, 2 * i + part + 1)
                dve.tensor_tensor(ms_lo[:, part, :, :], mix[:, i, 4 * part:4 * part + 4, :],
                                  ms_hi[:, part, :, :].bitcast(F32), ALU.subtract).then_inc(ms_lo_s, 1)

            def residual(i):
                dve.wait_ge(xres_loaded[i % 2], 16 * (i // 2 + 1))
                hrow = mix[:, i, :, :].rearrange("p k t -> p (k t)")
                for dh in range(2):
                    dve.wait_ge(wo_ready, 2 * i + dh + 1)
                    c = slice(dh * BANK, (dh + 1) * BANK)
                    dve.tensor_tensor(hrow[:, c], ps[:, (PJ, PV)[i % 2] + dh, :], hrow[:, c], ALU.add).then_inc(h_ready, 1)

            def norm_h(i):
                if i == 0:
                    dve.wait_ge(g2_loaded, 16)
                dve.wait_ge(h_rstd, i + 1)
                n = TILES + 1 + i
                dve.scalar_tensor_tensor(out=xn2[:, :], in0=mix[:, i, :, :].rearrange("p k t -> p (k t)"),
                                         scalar=rstd[:, n:n + 1], in1=g2b[:, :], op0=ALU.mult, op1=ALU.mult).then_inc(hn_ready, 1)

            def lo_h(i):
                dve.wait_ge(hhi_ready, i + 1)
                dve.tensor_tensor(hn2_lo[:, :, i * P:(i + 1) * P],
                                  ps[:, TB:TB + 2, :].rearrange("p b (k t) -> p (b k) t", k=4),
                                  hn2_hi[:, :, i * P:(i + 1) * P].bitcast(F32), ALU.subtract).then_inc(hlo_ready, 1)

            ln_stats(0)
            mix_lo(0, 0)
            ln_normalise(0)
            mix_lo(0, 1)
            for i in range(TILES):
                if i + 1 < TILES:
                    ln_stats(i + 1)
                    ln_normalise(i + 1)
                    mix_lo(i + 1, 0)
                if i >= 1:
                    norm_h(i - 1)
                if i + 1 < TILES:
                    mix_lo(i + 1, 1)
                if i >= 1:
                    lo_h(i - 1)
                residual(i)
            norm_h(TILES - 1)
            lo_h(TILES - 1)

            def products(f):
                for tg in range(2):
                    c = slice(tg * BANK, (tg + 1) * BANK)
                    dve.wait_ge(silu_done, 2 * f + tg + 1)
                    dve.wait_ge(u_ready2, 2 * f + tg + 1)
                    dve.wait_ge(act_lo_s, f)
                    dve.tensor_tensor(prod[:, c], sil[:, c], ps[:, Z + tg, :], ALU.mult).then_inc(prod_done, 1)

            def act_low(f, slot):
                dve.wait_ge(act_hi_s, f + 1)
                dve.tensor_tensor(act_lo[:, slot, :], prod[:, :], act_hi[:, slot, :].bitcast(F32),
                                  ALU.subtract).then_inc(act_lo_s, 1)

            def down(c):
                for i in range(TILES):
                    for dh in range(2):
                        n = 2 * i + dh
                        s = slice(dh * BANK, (dh + 1) * BANK)
                        hrow = mix[:, i, :, :].rearrange("p k t -> p (k t)")[:, s]
                        dve.wait_ge(d_ready, 16 * c + n + 1)
                        dve.wait_ge(d_added, 16 * c)
                        dve.tensor_tensor(hrow, ps[:, TB + n % 4, :], hrow, ALU.add).then_inc(d_added, 1)

            def ffn(c, first):
                f = 2 * c
                products(f)
                if not first:
                    down(c - 1)
                act_low(f, 0)
                products(f + 1)
                act_low(f + 1, 1)

            ffn(0, True)
            with dve.Fori(1, CHUNKS) as c:
                ffn(c, False)
            def norm_out(i):
                if i == 0:
                    dve.wait_ge(gf_loaded, 16)
                dve.wait_ge(o_rstd, i + 1)
                n = 2 * TILES + 1 + i
                dve.scalar_tensor_tensor(out=ost[:, i % 2, :], in0=mix[:, i, :, :].rearrange("p k t -> p (k t)"),
                                         scalar=rstd[:, n:n + 1], in1=gfb[:, :], op0=ALU.mult, op1=ALU.mult).then_inc(o_ready, 1)

            c = CHUNKS - 1
            for i in range(TILES):
                for dh in range(2):
                    n = 2 * i + dh
                    s = slice(dh * BANK, (dh + 1) * BANK)
                    hrow = mix[:, i, :, :].rearrange("p k t -> p (k t)")[:, s]
                    dve.wait_ge(d_ready, 16 * c + n + 1)
                    dve.wait_ge(d_added, 16 * c)
                    dve.tensor_tensor(hrow, ps[:, TB + n % 4, :], hrow, ALU.add).then_inc(d_added, 1)
                if i:
                    norm_out(i - 1)
            norm_out(TILES - 1)

        @block.tensor
        def _(pe):
            pe.wait_ge(consts, 9)
            pe.wait_ge(par_loaded, 64)
            for c in range(4):
                last = pe.transpose(ps[:, PJ, c * NP:(c + 1) * NP], par_nat[:, c * P:(c + 1) * P], ident[0:NP, 0:NP])
            last.then_inc(par_t, 1)

            def transpose_x(t):
                r = META if t == 0 else P
                b = (TB, Z)[t % 2]
                pe.wait_ge(xn_ready, t + 1)
                if t >= 2:
                    pe.wait_ge(xlo_ready, t - 1)
                for k in range(KD):
                    last = pe.transpose(ps[:, b + k // 4, (k % 4) * P:(k % 4) * P + r],
                                        xnorm[0:r, t % 2, k * P:(k + 1) * P], ident[0:r, 0:r])
                last.then_inc(xt_ready, 1)

            def project_v(b):
                c0 = min(b * P, T - P)
                if b == 0:
                    pe.wait_ge(wlo_done, 4)
                pe.wait_ge(xlo_ready, min(b + 2, TILES + 1))
                if b >= 2:
                    pe.wait_ge(v_copied, b - 1)
                hn, wv = (hn_hi, hn_lo), (wv_hi, wv_lo)
                for k in range(KD):
                    for s, m in PASSES:
                        last = pe.matmul(ps[:, PV + b % 2, :], hn[s][:, k, c0:c0 + P], wv[m][:, k, :],
                                         start=(k == 0 and s == m == 0), stop=(k == KD - 1 and s == 1))
                last.then_inc(v_ready, 1)

            for t in range(TILES + 1):
                transpose_x(t)
                if t >= 2:
                    project_v(t - 2)
            for b in range(TILES - 1, TILES + 1):
                project_v(b)

            def groups(p, which, loop):
                for kind, g in which:
                    idx = GROUPS.index((kind, g))
                    waits = []
                    if g == 0:
                        if not loop:
                            n = {"cg": CH_CG0, "ca": CH_CA0}[kind]
                        else:
                            n = {"k": CH_K0 + 4 * p, "q": CH_Q0 + 4 * p, "cg": CH_LOOP + 4 * p, "ca": CH_LOOP + 1 + 4 * p}[kind]
                        waits.append((wlo_done, n + 1))
                    if idx >= 2:
                        before = GROUPS[idx - 2]
                        if loop or idx - 2 >= FIRST:
                            waits.append(freed(*before, p))
                    else:
                        waits.append(freed(*GROUPS[9 + (idx + 1) % 2], p - 1))
                    if not loop and idx == FIRST:
                        waits.append((par_ready, 1))
                    slot = 0 if kind in ("k", "cg") else 1
                    c0, n = tok(kind, g)
                    for w in waits:
                        pe.wait_ge(*w)
                    w_, hn = (wp_hi, wp_lo), (hn_hi, hn_lo)
                    for k in range(KD):
                        for s, m in PASSES:
                            last = pe.matmul(ps[:, pj_bank(kind, g), 0:n], w_[s][:, slot, k, :], hn[m][:, k, c0:c0 + n],
                                             start=(k == 0 and s == m == 0), stop=(k == KD - 1 and s == 1))
                    last.then_inc(pj_ready, 1)

            groups(-1, GROUPS[FIRST:], False)

            def pair(p, more):
                groups(p, GROUPS if more else GROUPS[:FIRST], True)

                def scores(n):
                    h, i = UNITS[n]
                    if n == 0:
                        pe.wait_ge(k_dup, 16 * (p + 1))
                        pe.wait_ge(pj_free_dve, 3 + 8 * p + 5)
                    d0 = META + i * P
                    for c, (c0, cols, used) in enumerate(z_chunks(i)):
                        m = CZ[n] + c
                        pe.wait_ge(z_free, NZ * p + max(m - 1, 0))
                        for part in range(2):
                            last = pe.matmul(ps[:, Z + m % 2, 0:cols], qst[:, h, i * P:(i + 1) * P],
                                             kd[:, h, part, c0:c0 + cols], start=(part == 0),
                                             stop=(part == 1 and c0 + used <= d0))
                        lo, hi = max(d0, c0), c0 + used
                        if hi > lo:
                            last = pe.matmul(ps[:, Z + m % 2, lo - c0:hi - c0], ident_bf[:, :],
                                             mask_bf[:, lo - d0:hi - d0], start=False, stop=True)
                        last.then_inc(z_ready, 1)

                def transpose_w(n, banks):
                    h, i = UNITS[n]
                    for b in banks:
                        m = CT[n] + b
                        if b == 0:
                            pe.wait_ge(w_ready, NU * p + n + 1)
                            if i < 3:
                                pe.wait_ge(tail_zeroed, 6 * p + 3 * h + i + 1)
                        pe.wait_ge(t_copied, NT * p + max(m - 1, 0))
                        for j, kb in enumerate(t_banks(i)[b]):
                            last = pe.transpose(ps[:, TB + m % 2, j * P:(j + 1) * P],
                                                wbeta[:, n % 3, kb * P:(kb + 1) * P], ident[:, :])
                        last.then_inc(t_ready, 1)

                def attend(n):
                    h, i = UNITS[n]
                    g = n // 4
                    if n % 4 == 0:
                        pe.wait_ge(pv_evac, NG * p + max(g - 1, 0))
                    if n == 0:
                        pe.wait_ge(v_loaded, 32 * (p + 1))
                    for b, blocks in enumerate(t_banks(i)):
                        m = CT[n] + b
                        pe.wait_ge(t_copied, NT * p + m + 1)
                        for j, kb in enumerate(blocks):
                            last = pe.matmul(ps[DH * h:DH * h + DH, PV + g % 2, (i % 4) * P:(i % 4 + 1) * P],
                                             vs[:, kb, DH * h:DH * h + DH], w_t[:, m % 4, j, :],
                                             start=(kb == 0), stop=(kb == i + 1))
                        last.then_inc(pv_used, 1)

                scores(0)
                scores(1)
                for n in range(NU + 1):
                    if n + 2 < NU:
                        scores(n + 2)
                    if n < NU:
                        nb = len(t_banks(UNITS[n][1]))
                        transpose_w(n, range(min(2, nb)))
                    if n:
                        attend(n - 1)
                    if n < NU:
                        transpose_w(n, range(2, nb))

            with pe.Fori(0, PAIRS - 1) as p:
                pair(p, True)
            pair(PAIRS - 1, False)

            def ln_forward(i):
                if i == 0:
                    pe.wait_ge(conv_step, (CONV_K + 1) * PAIRS)
                else:
                    pe.wait_ge(ln_norm, i)
                for c in range(4):
                    last = pe.transpose(ps[:, Z, c * P:(c + 1) * P], mix[:, i, 4 + c, :], ident[:, :])
                last.then_inc(ln_t, 1)

            def ln_backward(i):
                pe.wait_ge(ln_norm, i + 1)
                pe.wait_ge(ln_silu, 4 * i)
                for c in range(4):
                    last = pe.transpose(ps[:, Z + 1, c * P:(c + 1) * P], mix[:, i, 4 + c, :], ident[:, :])
                last.then_inc(ln_back, 1)

            def w_out_part(i, part):
                if i == 0 and part == 0:
                    pe.wait_ge(wlo_done, CH_WO + KD)
                if i >= 2 and part == 0:
                    pe.wait_ge(h_ready, 2 * (i - 1))
                pe.wait_ge(ms_lo_s, 2 * i + part + 1)
                ms, wo = (ms_hi, ms_lo), (wo_hi, wo_lo)
                for dh in range(2):
                    for k in range(4):
                        for s, m in PASSES:
                            last = pe.matmul(ps[:, (PJ, PV)[i % 2] + dh, :], ms[s][:, part, k, :],
                                             wo[m][:, 4 * part + k, dh * BANK:(dh + 1) * BANK],
                                             start=(part == 0 and k == 0 and s == m == 0),
                                             stop=(part == 1 and k == 3 and s == 1))
                    if part:
                        last.then_inc(wo_ready, 1)
                if not part:
                    last.then_inc(ms_used, 1)

            def transpose_h(i):
                pe.wait_ge(hn_ready, i + 1)
                pe.wait_ge(hlo_ready, i)
                for k in range(KD):
                    last = pe.transpose(ps[:, TB + k // 4, (k % 4) * P:(k % 4 + 1) * P],
                                        xn2[:, k * P:(k + 1) * P], ident[:, :])
                last.then_inc(ht_ready, 1)

            ln_forward(0)
            ln_backward(0)
            for i in range(TILES):
                if i + 1 < TILES:
                    ln_forward(i + 1)
                w_out_part(i, 0)
                if i + 1 < TILES:
                    ln_backward(i + 1)
                if i >= 1:
                    transpose_h(i - 1)
                w_out_part(i, 1)
            transpose_h(TILES - 1)

            def gate_up(f, slot):
                hn2 = (hn2_hi, hn2_lo)
                pe.wait_ge(wlo_done, CH_GU + 2 * f + 2)
                for tg in range(2):
                    for n, (bank, s_, free) in enumerate(((PJ + tg, g_ready, silu_done), (Z + tg, u_ready2, prod_done))):
                        pe.wait_ge(free, 2 * f)
                        w_ = (gu_hi[slot], gu_lo[slot])
                        for k in range(KD):
                            for s, m in PASSES:
                                last = pe.matmul(ps[:, bank, :], w_[s][:, n, k, :],
                                                 hn2[m][:, k, tg * BANK:(tg + 1) * BANK],
                                                 start=(k == 0 and s == m == 0), stop=(k == KD - 1 and s == 1))
                        last.then_inc(s_, 1)

            def down(c, first):
                pe.wait_ge(act_lo_s, 2 * c + 2)
                pe.wait_ge(dlo_done, c + 1)
                a, w_ = (act_hi, act_lo), (wd_hi, wd_lo)
                for i in range(TILES):
                    for dh in range(2):
                        n = 2 * i + dh
                        if not (first and n < 4):
                            pe.wait_ge(d_added, 16 * c + n - 3)
                        for t in range(2):
                            for s, m in PASSES:
                                last = pe.matmul(ps[:, TB + n % 4, :], a[s][:, t, i * P:(i + 1) * P],
                                                 w_[m][:, t, dh * BANK:(dh + 1) * BANK],
                                                 start=(t == 0 and s == m == 0), stop=(t == 1 and s == 1))
                        last.then_inc(d_ready, 1)

            pe.wait_ge(hlo_ready, TILES)
            pe.wait_ge(h_ready, 2 * TILES)
            gate_up(0, 0)
            gate_up(1, 1)
            gate_up(2, 0)
            down(0, True)
            gate_up(3, 1)
            with pe.Fori(2, CHUNKS) as c:
                gate_up(2 * c, 0)
                down(c - 1, False)
                gate_up(2 * c + 1, 1)
            down(CHUNKS - 1, False)


_INS = ["x", "meta_tokens", "mix_norm_g", "w_in", "conv_dw_w", "conv_dw_b", "conv_ln_g", "conv_ln_b", "w_out",
        "ffn_norm_g", "w_gate", "w_up", "w_down", "final_norm_g"]


def kernel(**inputs):
    import numpy as np
    import concourse.bacc as bacc
    from concourse.bass_utils import run_bass_kernel_spmd

    nc = bacc.Bacc("TRN2", target_bir_lowering=False, num_devices=1)
    arrays, args = {}, []
    for name in _INS:
        a = np.ascontiguousarray(inputs[name])
        arrays[f"in_{name}"] = a
        args.append(nc.dram_tensor(f"in_{name}", a.shape, mybir.dt.from_np(a.dtype), kind="ExternalInput").ap())
    x = inputs["x"]
    out = nc.dram_tensor("out", x.shape, F32, kind="ExternalOutput").ap()
    tokens = x.shape[1] + inputs["meta_tokens"].shape[0]
    width = inputs["w_out"].shape[1] - inputs["conv_dw_w"].shape[2]
    v_dram = nc.dram_tensor("v_dram", (tokens, width), F32).ap()
    hybrid_block(nc, *args, out, v_dram)
    r = run_bass_kernel_spmd(nc, [arrays], core_ids=[0])
    return r.results[0]["out"]
```

```python
import math
from contextlib import ExitStack

import concourse.bass as bass
from concourse import mybir

F32 = mybir.dt.float32
F32R = mybir.dt.float32r
BF16 = mybir.dt.bfloat16
ALU = mybir.AluOpType
ACT = mybir.ActivationFunctionType

P = 128
BANK = 512
PASSES = ((0, 0), (0, 1), (1, 0))


def hybrid_block(nc, x, meta_tokens, mix_norm_g, w_in, conv_dw_w, conv_dw_b, conv_ln_g, conv_ln_b,
                 w_out, ffn_norm_g, w_gate, w_up, w_down, final_norm_g, out, v_dram):
    D = x.shape[2]
    L = x.shape[1]
    META = meta_tokens.shape[0]
    T = META + L
    KD = D // P
    TILES = L // P
    CONV_K, CH = conv_dw_w.shape[1], conv_dw_w.shape[2]
    FF = w_gate.shape[2]
    CHUNKS = FF // P // 2
    SB = w_out.shape[1] - CH
    DH = 64
    PAIRS = SB // (2 * DH)
    KB = T // P + 1
    PAD = CONV_K - 1 - META
    SCALE = 1.0 / math.sqrt(DH)
    EPS = 1e-6
    assert PAIRS == CH // P == 4 and TILES == 8 and KD == 8

    w_in_t = w_in[0].rearrange("(k p) c -> p k c", p=P)
    w_out_t = w_out[0].rearrange("(k p) c -> p k c", p=P)
    w_gate_t = w_gate[0].rearrange("(k p) c -> p k c", p=P)
    w_up_t = w_up[0].rearrange("(k p) c -> p k c", p=P)
    w_down_t = w_down[0].rearrange("(f p) c -> p f c", p=P)
    Q0, K0, V0, CA0, CG0 = 0, SB, 2 * SB, 3 * SB, 3 * SB + CH

    W3 = 2 * (-(-T // 6))
    ALL_TOKENS = [(g * W3, min(W3, T - g * W3)) for g in range(3)]
    OUT_TOKENS = [(META + g * BANK, BANK) for g in range(L // BANK)]

    UNITS = [(0, 1), (0, 2), (0, 0), (1, 0), (0, 7), (1, 1), (1, 7), (1, 2),
             (0, 6), (0, 3), (1, 6), (1, 3), (0, 5), (0, 4), (1, 5), (1, 4)]
    assert sorted(UNITS) == [(h, i) for h in range(2) for i in range(TILES)]

    def width(i):
        return META + P * (i + 1)

    def z_chunks(i):
        w = width(i)
        n = -(-w // BANK)
        c = max(2 * (-(-w // (2 * n))), 256)
        return [(a, min(c, max(w - a, 256)), min(c, w - a)) for a in range(0, w, c)]

    def t_banks(i):
        nb = i + 2
        return [range(a, min(a + 4, nb)) for a in range(0, nb, 4)]

    def counted(f):
        c = [0]
        for _, i in UNITS:
            c.append(c[-1] + len(f(i)))
        return c

    CZ, CT = counted(z_chunks), counted(t_banks)
    NZ, NT, NU, NG = CZ[-1], CT[-1], len(UNITS), 2
    assert CZ[2] == 2 and NT % 4 == 0
    FIRST_HALF = max(n for n, (_, i) in enumerate(UNITS) if i < TILES // 2)

    GROUPS = ([("k", g) for g in range(3)] + [("q", g) for g in range(2)]
              + [("cg", g) for g in range(3)] + [("ca", g) for g in range(3)])
    FIRST = 5
    DVE_G = {("k", g): g for g in range(3)} | {("q", g): 3 + g for g in range(2)} | {("ca", g): 5 + g for g in range(3)}
    NP = CONV_K + 3

    ctx = ExitStack()
    with ctx:
        def sem(name):
            return ctx.enter_context(nc.semaphore(name))

        def region(name, size, *stages):
            found = []
            for tensors in stages:
                with ExitStack() as stack:
                    for n, shape, dt in tensors:
                        found.append(stack.enter_context(nc.sbuf_tensor(n, shape, dt)))
            ctx.enter_context(nc.sbuf_tensor(name, [P, size], F32))
            return found

        (hn_hi, hn_lo, wo_lo, wo_hi, wo_raw, gu1_hi, gu1_lo, wd_hi, wd_lo, wd_raw, act_hi, act_lo, sil, prod) = region(
            "region1", 2 * KD * T,
            [("hn_hi", [P, KD, T], F32R), ("hn_lo", [P, KD, T], F32R)],
            [("wo_lo", [P, KD, D], F32R), ("wo_hi", [P, KD, D], F32R)],
            [("wo_raw", [P, KD, D], F32)],
            [("gu1_hi", [P, 2, KD, P], F32R), ("gu1_lo", [P, 2, KD, P], F32R),
             ("wd_hi", [P, 2, D], F32R), ("wd_lo", [P, 2, D], F32R), ("wd_raw", [P, 2, D], F32),
             ("act_hi", [P, 2, L], F32R), ("act_lo", [P, 2, L], F32R),
             ("sil", [P, L], F32), ("prod", [P, L], F32)])
        (xin, xnorm, g1b, v_stage, qst, kd, wbeta, gq, w_t, vs, hn2_hi, hn2_lo) = region(
            "region2", 2 * KD * L,
            [("xin", [P, 2, D], F32), ("xnorm", [P, 2, D], F32), ("g1b", [P, D], F32),
             ("v_stage", [P, 2, SB], F32)],
            [("qst", [P, 2, L], F32R), ("kd", [P, 2, 2, T], F32R), ("wbeta", [P, 3, KB * P], F32),
             ("gq", [P, 3, T], F32), ("w_t", [P, 4, 4, P], F32), ("vs", [P, KB, P], F32)],
            [("hn2_hi", [P, KD, L], F32R), ("hn2_lo", [P, KD, L], F32R)])
        (wv_hi, wv_lo, mix) = region(
            "region3", KD * L,
            [("wv_hi", [P, KD, SB], F32R), ("wv_lo", [P, KD, SB], F32R)],
            [("mix", [P, TILES, KD, P], F32)])
        (wp_hi, wp_lo, ms_hi, ms_lo, xn2, g2b, ost, gfb) = region(
            "region4", 4 * KD * P,
            [("wp_hi", [P, 2, KD, P], F32R), ("wp_lo", [P, 2, KD, P], F32R)],
            [("ms_hi", [P, 2, 4, P], F32R), ("ms_lo", [P, 2, 4, P], F32R), ("xn2", [P, D], F32),
             ("g2b", [P, D], F32)],
            [("ost", [P, 2, D], F32), ("gfb", [P, D], F32)])
        (par_nat, u_pad, u_next, acc, gu0_hi, gu0_lo) = region(
            "region5", PAD + 2 * T + 2 * L,
            [("par_nat", [NP, CH], F32)],
            [("u_pad", [P, PAD + T], F32), ("u_next", [P, T], F32), ("acc", [P, 2, L], F32)],
            [("gu0_hi", [P, 2, KD, P], F32R), ("gu0_lo", [P, 2, KD, P], F32R)])

        def keep(name, shape, dt):
            return ctx.enter_context(nc.sbuf_tensor(name, shape, dt))

        raw = keep("raw", [P, 2, KD * P], F32)
        ones = keep("ones", [P, 1], F32)
        zeros = keep("zeros", [P, 1], F32)
        ident = keep("ident", [P, P], F32)
        ident_bf = keep("ident_bf", [P, P], BF16)
        mask_bf = keep("mask_bf", [P, P], BF16)
        par = keep("par", [P, 4, NP], F32)
        parp = keep("parp", [P, NP], F32)
        half = keep("half", [P, 1], F32)
        sumsq = keep("sumsq", [P, 3 * (TILES + 1)], F32)
        var = keep("var", [P, 3 * (TILES + 1)], F32)
        rstd = keep("rstd", [P, 3 * (TILES + 1)], F32)
        bn6 = keep("bn6", [P, 6], F32)
        bn2 = keep("bn2", [P, 2 * TILES], F32)
        ln_var = keep("ln_var", [P, TILES], F32)
        ln_rstd = keep("ln_rstd", [P, TILES], F32)

        ps = ctx.enter_context(nc.psum_tensor("ps", [P, 8, BANK], F32))
        PJ, Z, TB, PV = 0, 2, 4, 6

        gu_hi, gu_lo = [gu0_hi, gu1_hi], [gu0_lo, gu1_lo]

        par_loaded, g1_loaded, g2_loaded, gf_loaded = sem("par_loaded"), sem("g1_loaded"), sem("g2_loaded"), sem("gf_loaded")
        x_loaded = [sem("x_loaded0"), sem("x_loaded1")]
        consts, par_t, par_ready = sem("consts"), sem("par_t"), sem("par_ready")
        x_sumsq, x_var, x_rstd, xn_ready = sem("x_sumsq"), sem("x_var"), sem("x_rstd"), sem("xn_ready")
        xt_ready, xhi_ready, xlo_ready = sem("xt_ready"), sem("xhi_ready"), sem("xlo_ready")
        raw_loaded = [sem("raw_loaded0"), sem("raw_loaded1")]
        whi_done, wlo_done = sem("whi_done"), sem("wlo_done")
        v_ready, v_copied = sem("v_ready"), sem("v_copied")
        v_stored = [sem("v_stored0"), sem("v_stored1")]
        pj_ready, pj_free_dve, pj_free_act = sem("pj_ready"), sem("pj_free_dve"), sem("pj_free_act")
        pj_hi = sem("pj_hi")
        k_dup, v_loaded, v_zeroed = sem("k_dup"), sem("v_loaded"), sem("v_zeroed")
        u_zeroed, u_ready, conv_step = sem("u_zeroed"), sem("u_ready"), sem("conv_step")
        z_ready, z_free, scanned, w_ready = sem("z_ready"), sem("z_free"), sem("scanned"), sem("w_ready")
        tail_zeroed, t_ready, t_copied, pv_used, pv_evac = sem("tail_zeroed"), sem("t_ready"), sem("t_copied"), sem("pv_used"), sem("pv_evac")
        ln_t, ln_stat, ln_agg, ln_var_s, ln_rstd_s, ln_norm = sem("ln_t"), sem("ln_stat"), sem("ln_agg"), sem("ln_var_s"), sem("ln_rstd_s"), sem("ln_norm")
        ln_back, ln_silu, ms_hi_s, ms_lo_s, ms_used = sem("ln_back"), sem("ln_silu"), sem("ms_hi_s"), sem("ms_lo_s"), sem("ms_used")
        wo_loaded = [sem(f"wo_loaded{n}") for n in range(4)]
        wo_hi_s, wo_lo_s = sem("wo_hi_s"), sem("wo_lo_s")
        wo_ready, h_ready = sem("wo_ready"), sem("h_ready")
        xres_loaded = [sem("xres_loaded0"), sem("xres_loaded1")]
        h_sumsq, h_var, h_rstd, hn_ready = sem("h_sumsq"), sem("h_var"), sem("h_rstd"), sem("hn_ready")
        ht_ready, hhi_ready, hlo_ready = sem("ht_ready"), sem("hhi_ready"), sem("hlo_ready")
        wd_loaded, dhi_done, dlo_done = sem("wd_loaded"), sem("dhi_done"), sem("dlo_done")
        g_ready, u_ready2, silu_done, prod_done = sem("g_ready"), sem("u_ready2"), sem("silu_done"), sem("prod_done")
        act_hi_s, act_lo_s, d_ready, d_added = sem("act_hi_s"), sem("act_lo_s"), sem("d_ready"), sem("d_added")
        o_sumsq, o_var, o_rstd, o_ready = sem("o_sumsq"), sem("o_var"), sem("o_rstd"), sem("o_ready")
        o_stored = [sem("o_stored0"), sem("o_stored1")]

        def past(n):
            return n + 1

        WO_AT = 6
        HELD_BACK = 2
        EARLY = 8

        block = ctx.enter_context(nc.Block())

        CH_V, CH_CG0, CH_CA0, CH_K0, CH_Q0 = 0, 4, 5, 6, 7
        CH_LOOP = 8
        CH_GU = CH_LOOP + 4 * (PAIRS - 1)

        def pj_bank(kind, g):
            return PJ + GROUPS.index((kind, g)) % 2

        def pj_count(kind, g, p):
            return 6 + 11 * p + GROUPS.index((kind, g)) + 1

        Z_BANKS = [(Z, Z + 1, PJ + 1, PJ)[m % 4] for m in range(NZ)]
        for m in range(NZ - 6, NZ):
            Z_BANKS[m] = (Z, Z + 1, PJ + 1)[m % 3]

        def z_before(m):
            return max((n + 1 for n in range(m) if Z_BANKS[n] == Z_BANKS[m]), default=0)

        def used_up(kind, p):
            return pj_ready, pj_count(kind, 1 if kind == "q" else 2, p)

        def freed(kind, g, p):
            if kind == "cg":
                return pj_free_act, 3 + 3 * p + g + 1
            return pj_free_dve, 3 + 8 * p + DVE_G[kind, g] + 1

        MS_ORDER = [(0, 0), (1, 0)] + [t for i in range(TILES) for t in ((i, 1), (i + 2, 0)) if t[0] < TILES]

        def ms_count(i, part):
            return MS_ORDER.index((i, part)) + 1

        def tok(kind, g):
            return OUT_TOKENS[g] if kind == "q" else ALL_TOKENS[g]

        def chunk_loaded(j):
            return raw_loaded[j % 2], 16 * (j // 2 + 1)

        @block.sync
        def _(sp):
            def load_x(t):
                if t >= 2:
                    sp.wait_ge(xn_ready, t - 1)
                if t == 0:
                    sp.dma_start(xin[0:META, 0, :], meta_tokens).then_inc(x_loaded[0], 16)
                else:
                    sp.dma_start(xin[:, t % 2, :], x[0, (t - 1) * P:t * P, :]).then_inc(x_loaded[t % 2], 16)

            def load_chunk(j, dst, src, slot=None):
                sp.wait_ge(wlo_done, j - 1)
                sp.dma_start(dst, src).then_inc(raw_loaded[slot], 16)

            def tile_of(slot):
                return raw[:, slot, :].rearrange("p (k c) -> p k c", k=KD)

            def load_tile(j, slot, src_t, col):
                load_chunk(j, tile_of(slot), src_t[:, :, bass.ds(col, P)], slot)

            load_x(0)
            load_x(1)
            sp.dma_start(g1b[:, :], mix_norm_g[0].partition_broadcast(P)).then_inc(g1_loaded, 16)
            for j in range(4):
                if j < 2:
                    sp.dma_start(raw[:, j, :].rearrange("p (k c) -> p k c", k=2),
                                 w_in_t[:, 2 * j:2 * j + 2, V0:V0 + SB]).then_inc(raw_loaded[j], 16)
                else:
                    load_chunk(j, raw[:, j % 2, :].rearrange("p (k c) -> p k c", k=2),
                               w_in_t[:, 2 * j:2 * j + 2, V0:V0 + SB], j % 2)
                load_x(2 + j)
            sp.dma_start(par_nat[0:CONV_K, :], conv_dw_w[0]).then_inc(par_loaded, 16)
            for n, v in enumerate((conv_dw_b, conv_ln_g, conv_ln_b)):
                sp.dma_start(par_nat[CONV_K + n:CONV_K + n + 1, :], v[0:1, :]).then_inc(par_loaded, 16)
            for t in range(6, TILES + 1):
                load_x(t)
            load_tile(CH_CG0, 0, w_in_t, CG0)
            load_tile(CH_CA0, 1, w_in_t, CA0)
            load_tile(CH_K0, 0, w_in_t, K0)
            load_tile(CH_Q0, 1, w_in_t, Q0)
            sp.wait_ge(v_stored[0], 16 * 5)
            sp.wait_ge(v_stored[1], 16 * 4)
            sp.wait_ge(v_zeroed, 1)

            def pair_loads(p, more):
                if more:
                    load_tile(CH_LOOP + 4 * p, 0, w_in_t, CG0 + P * (p + 1))
                    load_tile(CH_LOOP + 4 * p + 1, 1, w_in_t, CA0 + P * (p + 1))
                sp.wait_ge(pv_used, past(NT * p))
                FB = T // P
                sp.dma_start(vs[:, 0:FB, :], v_dram[0:FB * P, bass.ds(P * p, P)].rearrange(
                    "(b p) c -> p b c", p=P)).then_inc(v_loaded, 16)
                sp.dma_start(vs[0:T - FB * P, FB, :], v_dram[FB * P:T, bass.ds(P * p, P)]).then_inc(v_loaded, 16)
                sp.wait_ge(pj_free_dve, 3 + 8 * p + 3)
                sp.dma_start(kd[DH:2 * DH, :, :, :].bitcast(F32), kd[0:DH, :, :, :].bitcast(F32)).then_inc(k_dup, 16)
                if more:
                    load_tile(CH_LOOP + 4 * p + 2, 0, w_in_t, K0 + P * (p + 1))
                    load_tile(CH_LOOP + 4 * p + 3, 1, w_in_t[:, :, Q0 + P:Q0 + SB], P * p)

            with sp.Fori(0, PAIRS - 1) as p:
                pair_loads(p, True)
            pair_loads(PAIRS - 1, False)
            sp.wait_ge(*used_up("q", PAIRS - 1))
            for n in range(4):
                ks = slice(2 * n, 2 * n + 2)
                sp.dma_start(wo_raw[:, ks, :], w_out_t[:, ks, :]).then_inc(wo_loaded[n], 16)
            sp.dma_start(g2b[:, :], ffn_norm_g[0].partition_broadcast(P)).then_inc(g2_loaded, 16)
            load_tile(CH_GU, 0, w_gate_t, 0)
            load_tile(CH_GU + 1, 1, w_up_t, 0)
            for i in range(TILES):
                sp.wait_ge(ms_lo_s, ms_count(i, 1))
                sp.dma_start(mix[:, i, :, :].rearrange("p k t -> p (k t)"),
                             x[0, i * P:(i + 1) * P, :]).then_inc(xres_loaded[i % 2], 16)
            sp.wait_ge(wo_ready, 2 * TILES)
            sp.wait_ge(ht_ready, TILES)
            sp.dma_start(gfb[:, :], final_norm_g.partition_broadcast(P)).then_inc(gf_loaded, 16)

            def ffn_loads(c, more):
                f = 2 * c
                load_tile(CH_GU + 2 * f + 2, 0, w_gate_t, P * (f + 1))
                load_tile(CH_GU + 2 * f + 3, 1, w_up_t, P * (f + 1))
                sp.wait_ge(dlo_done, past(c))
                sp.dma_start(wd_raw[:, :, :], w_down_t[:, bass.ds(f, 2), :]).then_inc(wd_loaded, 16)
                if more:
                    load_tile(CH_GU + 2 * f + 4, 0, w_gate_t, P * (f + 2))
                    load_tile(CH_GU + 2 * f + 5, 1, w_up_t, P * (f + 2))

            with sp.Fori(0, CHUNKS - 1) as c:
                ffn_loads(c, True)
            ffn_loads(CHUNKS - 1, False)
            for i in range(TILES):
                sp.wait_ge(o_ready, i + 1)
                sp.dma_start(out[0, i * P:(i + 1) * P, :], ost[:, i % 2, :]).then_inc(o_stored[i % 2], 16)
            for s in o_stored:
                sp.wait_ge(s, 16 * TILES // 2)

        @block.gpsimd
        def _(pool):
            pool.sem_inc(dlo_done, 1)
            pool.memset(ident[:, :], 0.0).then_inc(consts, 1)
            pool.memset(ident_bf[:, :], 0.0).then_inc(consts, 1)
            pool.memset(mask_bf[:, :], -1e30).then_inc(consts, 1)
            pool.memset(half[:, :], -0.5).then_inc(consts, 1)
            pool.memset(ones[:, :], 1.0).then_inc(consts, 1)
            pool.memset(zeros[:, :], 0.0).then_inc(consts, 1)
            pool.wait_ge(consts, 6)
            pool.affine_select(out=ident[:, :], in_=ident[:, :], compare_op=ALU.not_equal, fill=1.0,
                               base=0, pattern=[[-1, P]], channel_multiplier=1).then_inc(consts, 1)
            pool.affine_select(out=ident_bf[:, :], in_=ident_bf[:, :], compare_op=ALU.not_equal, fill=1.0,
                               base=0, pattern=[[-1, P]], channel_multiplier=1).then_inc(consts, 1)
            pool.affine_select(out=mask_bf[:, :], in_=mask_bf[:, :], compare_op=ALU.is_ge, fill=0.0,
                               base=0, pattern=[[1, P]], channel_multiplier=-1).then_inc(consts, 1)

            def root(src, v, dst, scale, ready, n, v_sem, r_sem):
                pool.wait_ge(ready, n)
                pool.tensor_scalar(v, src, scale, EPS, ALU.mult, ALU.add).then_inc(v_sem, 1)
                pool.wait_ge(v_sem, n)
                rows = src.shape[0]
                pool.tensor_tensor(dst, v, half[0:rows, :], ALU.pow).then_inc(r_sem, 1)

            def x_root(t):
                r = META if t == 0 else P
                root(sumsq[0:r, t:t + 1], var[0:r, t:t + 1], rstd[0:r, t:t + 1], 1.0 / D, x_sumsq, t + 1, x_var, x_rstd)

            def lo(j, slot, dst, hi):
                pool.wait_ge(whi_done, j + 1)
                pool.tensor_tensor(dst, raw[:, slot, :], hi.bitcast(F32), ALU.subtract).then_inc(wlo_done, 1)

            def wp(t, slot):
                return t[:, slot, :, :].rearrange("p k c -> p (k c)")

            def wv(t, j):
                return t[:, 2 * j:2 * j + 2, :].rearrange("p k c -> p (k c)")

            x_root(0)
            x_root(1)
            for t in range(2, TILES + 1):
                if t < 6:
                    lo(t - 2, t % 2, wv(wv_lo, t - 2), wv(wv_hi, t - 2))
                x_root(t)
            for j in (CH_CG0, CH_CA0):
                lo(j, j % 2, wp(wp_lo, j % 2), wp(wp_hi, j % 2))
            pool.wait_ge(par_ready, 1)
            pool.memset(u_pad[:, 0:PAD], 0.0).then_inc(u_zeroed, 1)
            for j in (CH_K0, CH_Q0):
                lo(j, j % 2, wp(wp_lo, j % 2), wp(wp_hi, j % 2))
            pool.wait_ge(xlo_ready, TILES + 1)
            pool.wait_ge(v_stored[0], 16 * 5)
            pool.wait_ge(v_stored[1], 16 * 4)
            pool.memset(vs[:, KB - 1, :], 0.0).then_inc(v_zeroed, 1)

            def w_out_lo(k):
                pool.wait_ge(wo_hi_s, k + 1)
                pool.tensor_tensor(wo_lo[:, k, :], wo_raw[:, k, :], wo_hi[:, k, :].bitcast(F32),
                                   ALU.subtract).then_inc(wo_lo_s, 1)

            def pair(p, more):
                if more:
                    for n in range(2):
                        lo(CH_LOOP + 4 * p + n, n, wp(wp_lo, n), wp(wp_hi, n))
                for n, (h, i) in enumerate(UNITS):
                    pool.wait_ge(t_ready, past(NT * p + (CT[n - 2] if n >= 3 else 0)))
                    gap = slice(width(i), P * (i + 2))
                    zero = zeros[:, :].broadcast_to([P, gap.stop - gap.start])
                    pool.tensor_tensor(wbeta[:, n % 3, gap], zero, zero, ALU.mult).then_inc(tail_zeroed, 1)
                    if n == 4 and more:
                        for m in (2, 3):
                            lo(CH_LOOP + 4 * p + m, m % 2, wp(wp_lo, m % 2), wp(wp_hi, m % 2))
                    if not more and n >= WO_AT + 2:
                        w_out_lo(n - WO_AT - 2)

            with pool.Fori(0, PAIRS - 1) as p:
                pair(p, True)
            pair(PAIRS - 1, False)
            def ln_root(i):
                pool.wait_ge(ln_agg, i + 1)
                pool.tensor_scalar(ln_var[:, i:i + 1], bn2[:, 2 * i + 1:2 * i + 2], 1.0, EPS, ALU.mult, ALU.add).then_inc(ln_var_s, 1)
                pool.wait_ge(ln_var_s, i + 1)
                pool.tensor_tensor(ln_rstd[:, i:i + 1], ln_var[:, i:i + 1], half[:, :], ALU.pow).then_inc(ln_rstd_s, 1)

            def h_root(i):
                n = TILES + 1 + i
                root(sumsq[:, n:n + 1], var[:, n:n + 1], rstd[:, n:n + 1], 1.0 / D, h_sumsq, i + 1, h_var, h_rstd)

            for k in range(NU - WO_AT - 2, 4):
                w_out_lo(k)
            ln_root(0)
            for k in range(max(4, NU - WO_AT - 2), KD):
                w_out_lo(k)
            for i in range(TILES):
                if i + 1 < TILES:
                    ln_root(i + 1)
                if i >= 1:
                    h_root(i - 1)
                if i == 3:
                    for n in range(2):
                        lo(CH_GU + n, n, wp(gu0_lo, n), wp(gu0_hi, n))
            h_root(TILES - 1)

            def ffn(c, more):
                f = 2 * c
                for n in range(2):
                    lo(CH_GU + 2 * f + 2 + n, n, wp(gu1_lo, n), wp(gu1_hi, n))
                if more:
                    for n in range(2):
                        lo(CH_GU + 2 * f + 4 + n, n, wp(gu0_lo, n), wp(gu0_hi, n))
                pool.wait_ge(dhi_done, c + 1)
                pool.tensor_tensor(wd_lo[:, :, :], wd_raw[:, :, :], wd_hi[:, :, :].bitcast(F32), ALU.subtract).then_inc(dlo_done, 1)

            with pool.Fori(0, CHUNKS - 1) as c:
                ffn(c, True)
            ffn(CHUNKS - 1, False)
            for i in range(TILES):
                n = 2 * TILES + 1 + i
                root(sumsq[:, n:n + 1], var[:, n:n + 1], rstd[:, n:n + 1], 1.0 / D, o_sumsq, i + 1, o_var, o_rstd)

        @block.scalar
        def _(act):
            def hi(j, slot, dst, wait=None):
                if wait:
                    act.wait_ge(*wait)
                act.wait_ge(raw_loaded[slot], 8 * (j - slot) + 16)
                act.activation(dst, raw[:, slot, :], ACT.Copy).then_inc(whi_done, 1)

            def wp(slot):
                return wp_hi[:, slot, :, :].rearrange("p k c -> p (k c)")

            def square_x(t):
                r = META if t == 0 else P
                act.wait_ge(x_loaded[t % 2], 16 * (t // 2 + 1))
                if t >= 2:
                    act.wait_ge(xt_ready, t - 1)
                act.activation(xnorm[0:r, t % 2, :], xin[0:r, t % 2, :], ACT.Square,
                               accum_out=sumsq[0:r, t:t + 1]).then_inc(x_sumsq, 1)

            def evac_x(t):
                n, c0 = (META, 0) if t == 0 else (P, META + (t - 1) * P)
                act.wait_ge(xt_ready, t + 1)
                b = (TB, Z)[t % 2]
                act.activation(hn_hi[:, :, c0:c0 + n],
                               ps[:, b:b + 2, :].rearrange("p b (k n) -> p (b k) n", k=4)[:, :, 0:n],
                               ACT.Copy).then_inc(xhi_ready, 1)

            def copy_v(b):
                act.wait_ge(v_ready, b + 1)
                if b >= 2:
                    act.wait_ge(v_stored[b % 2], 16 * (b // 2))
                act.activation(v_stage[:, b % 2, :], ps[:, PV + b % 2, :], ACT.Copy).then_inc(v_copied, 1)
                act.wait_ge(v_copied, b + 1)
                if b < T // P:
                    act.dma_start(v_dram[b * P:(b + 1) * P, :], v_stage[:, b % 2, :]).then_inc(v_stored[b % 2], 16)
                else:
                    n = T - b * P
                    act.dma_start(v_dram[b * P:T, :], v_stage[P - n:P, b % 2, :]).then_inc(v_stored[b % 2], 16)

            for s in (z_free, t_copied, pv_evac):
                act.sem_inc(s, 1)
            square_x(0)
            square_x(1)
            for t in range(TILES + 1):
                if t < 4:
                    j = t
                    hi(j, j % 2, wv_hi[:, 2 * j:2 * j + 2, :].rearrange("p k c -> p (k c)"))
                evac_x(t)
                if t + 2 <= TILES:
                    square_x(t + 2)
                if t == 7:
                    hi(CH_CG0, 0, wp(0))
                if t == 8:
                    hi(CH_CA0, 1, wp(1))
                if t >= 3:
                    copy_v(t - 3)

            def sigmoid_gate(p):
                for g, (c0, n) in enumerate(ALL_TOKENS):
                    act.wait_ge(pj_ready, pj_count("cg", g, p))
                    act.activation(u_next[:, c0:c0 + n], ps[:, pj_bank("cg", g), 0:n], ACT.Sigmoid).then_inc(pj_free_act, 1)

            def conv_input(p):
                act.wait_ge(conv_step, past((CONV_K + 1) * p))
                act.wait_ge(pj_free_dve, 3 + 8 * p)
                act.activation(parp[:, :], par[:, bass.ds(p, 1), :].rearrange("p a c -> p (a c)"), ACT.Copy).then_inc(u_ready, 1)
                act.activation(u_pad[:, PAD:PAD + T], u_next[:, :], ACT.Copy).then_inc(u_ready, 1)

            act.wait_ge(par_ready, 1)
            sigmoid_gate(-1)
            act.wait_ge(u_zeroed, 1)
            hi(CH_K0, 0, wp(0), used_up("cg", -1))
            conv_input(0)
            hi(CH_Q0, 1, wp(1), used_up("ca", -1))
            for b in range(TILES - 2, TILES + 1):
                copy_v(b)
            act.wait_ge(v_stored[0], 16 * 5)
            act.wait_ge(v_stored[1], 16 * 4)
            act.wait_ge(xlo_ready, TILES + 1)

            def split_hi(kind, g, p):
                c0, n = tok(kind, g)
                act.wait_ge(pj_ready, pj_count(kind, g, p))
                if g == 0:
                    act.wait_ge(z_ready, past(NZ * p))
                for h in range(2):
                    dst = kd[0:DH, h, 0, c0:c0 + n] if kind == "k" else qst[0:DH, h, g * BANK:(g + 1) * BANK]
                    act.activation(dst, ps[DH * h:DH * h + DH, pj_bank(kind, g), 0:n], ACT.Copy).then_inc(pj_hi, 1)

            def mix_hi(i, part):
                if i and part == 0:
                    act.wait_ge(ms_used, i)
                if i and part == 1:
                    act.wait_ge(wo_ready, 2 * i)
                if part:
                    act.wait_ge(ln_silu, 4 * (i + 1))
                act.activation(ms_hi[:, part, :, :], mix[:, i, 4 * part:4 * part + 4, :], ACT.Copy).then_inc(ms_hi_s, 1)

            def pair(p, more):
                for g in range(3):
                    split_hi("k", g, p)
                if more:
                    hi(CH_LOOP + 4 * p, 0, wp(0), used_up("k", p))
                split_hi("q", 0, p)
                if more:
                    split_hi("q", 1, p)
                    hi(CH_LOOP + 4 * p + 1, 1, wp(1), used_up("q", p))
                    act.wait_ge(u_ready, 2 * p + 2)
                    sigmoid_gate(p)
                    hi(CH_LOOP + 4 * p + 2, 0, wp(0), used_up("cg", p))

                def sigmoids(n):
                    h, i = UNITS[n]
                    act.wait_ge(t_ready, past(NT * p + (CT[n - 2] if n >= 3 else 0)))
                    chunks = z_chunks(i)
                    for c, (c0, _, used) in enumerate(chunks):
                        m = CZ[n] + c
                        act.wait_ge(z_ready, past(NZ * p + m + 1))
                        zp = ps[:, Z_BANKS[m], 0:used]
                        act.activation(gq[:, n % 3, c0:c0 + used], zp, ACT.Sigmoid, scale=-SCALE)
                        act.activation(wbeta[:, n % 3, c0:c0 + used], zp, ACT.Sigmoid, scale=SCALE).then_inc(z_free, 1)

                def copy_t(n):
                    for b, blocks in enumerate(t_banks(UNITS[n][1])):
                        m = CT[n] + b
                        act.wait_ge(t_ready, past(NT * p + m + 1))
                        act.wait_ge(pv_used, past(NT * p + max(m - 3, 0)))
                        c = len(blocks) * P
                        act.activation(w_t[:, m % 4, 0:len(blocks), :].rearrange("p b t -> p (b t)"),
                                       ps[:, TB + m % 2, 0:c], ACT.Copy).then_inc(t_copied, 1)

                def evac_attention(g, n):
                    act.wait_ge(pv_used, past(NT * p + CT[n + 1]))
                    act.activation(mix[:, 4 * g:4 * g + 4, bass.ds(p, 1), :].rearrange("p i a t -> p i (a t)"),
                                   ps[:, PV + g, :].rearrange("p (i t) -> p i t", i=4),
                                   ACT.Copy).then_inc(pv_evac, 1)

                sigmoids(0)
                sigmoids(1)
                if not more:
                    split_hi("q", 1, p)
                for n in range(NU):
                    if n + 2 < NU:
                        sigmoids(n + 2)
                    copy_t(n)
                    if n == 2 and more:
                        hi(CH_LOOP + 4 * p + 3, 1, wp(1), used_up("ca", p))
                    if n == 5 and more:
                        conv_input(p + 1)
                    if n == FIRST_HALF + 2:
                        evac_attention(0, FIRST_HALF)
                        if not more:
                            act.wait_ge(pv_evac, past(NG * PAIRS - 1))
                            mix_hi(0, 0)
                    if not more and WO_AT <= n < WO_AT + KD:
                        k = n - WO_AT
                        act.wait_ge(wo_loaded[k // 2], 16)
                        act.activation(wo_hi[:, k, :], wo_raw[:, k, :], ACT.Copy).then_inc(wo_hi_s, 1)
                if not more:
                    mix_hi(1, 0)
                evac_attention(1, NU - 1)

            with act.Fori(0, PAIRS - 1) as p:
                pair(p, True)
            pair(PAIRS - 1, False)

            def ln_silu_of(i):
                act.wait_ge(ln_back, i + 1)
                for c in range(4):
                    act.activation(mix[:, i, 4 + c, :], ps[:, Z + 1, c * P:(c + 1) * P], ACT.Silu,
                                   bias=par[:, c, CONV_K + 2:CONV_K + 3],
                                   scale=par[:, c, CONV_K + 1:CONV_K + 2]).then_inc(ln_silu, 1)

            def square_h(i):
                act.wait_ge(h_ready, 2 * (i + 1))
                if i:
                    act.wait_ge(ht_ready, i)
                act.activation(xn2[:, :], mix[:, i, :, :].rearrange("p k t -> p (k t)"), ACT.Square,
                               accum_out=sumsq[:, TILES + 1 + i:TILES + 2 + i]).then_inc(h_sumsq, 1)

            def evac_h(i):
                act.wait_ge(ht_ready, i + 1)
                act.activation(hn2_hi[:, :, i * P:(i + 1) * P],
                               ps[:, TB:TB + 2, :].rearrange("p b (k t) -> p (b k) t", k=4), ACT.Copy).then_inc(hhi_ready, 1)

            act.wait_ge(pv_evac, past(NG * PAIRS))
            for i in range(TILES):
                ln_silu_of(i)
                mix_hi(i, 1)
                if i >= 1:
                    square_h(i - 1)
                if i + 2 < TILES:
                    mix_hi(i + 2, 0)
                if i == 2:
                    act.wait_ge(conv_step, past((CONV_K + 1) * PAIRS))
                    for n in range(2):
                        hi(CH_GU + n, n, gu0_hi[:, n, :, :].rearrange("p k c -> p (k c)"))
                if i >= 1:
                    evac_h(i - 1)
            square_h(TILES - 1)
            evac_h(TILES - 1)

            act.wait_ge(wo_ready, 2 * TILES)

            def ffn_hi(j, n, dst, wait):
                hi(j, n, dst[:, n, :, :].rearrange("p k c -> p (k c)"), wait)

            def silu(f):
                for tg in range(2):
                    act.wait_ge(g_ready, 2 * f + tg + 1)
                    act.wait_ge(prod_done, 2 * f)
                    act.activation(sil[:, tg * BANK:(tg + 1) * BANK], ps[:, PJ + tg, :], ACT.Silu).then_inc(silu_done, 1)

            def act_split(f, slot, before):
                act.wait_ge(d_ready, before)
                act.wait_ge(prod_done, 2 * f + 2)
                act.activation(act_hi[:, slot, :], prod[:, :], ACT.Copy).then_inc(act_hi_s, 1)

            def ffn(c, first, more):
                f = 2 * c
                for n in range(2):
                    ffn_hi(CH_GU + 2 * f + 2 + n, n, gu1_hi, None if first else (u_ready2, 2 * f))
                silu(f)
                if more:
                    for n in range(2):
                        ffn_hi(CH_GU + 2 * f + 4 + n, n, gu0_hi, (u_ready2, 2 * f + 2))
                act_split(f, 0, 16 * c)
                act.wait_ge(wd_loaded, 16 * (c + 1))
                act.activation(wd_hi[:, :, :], wd_raw[:, :, :], ACT.Copy).then_inc(dhi_done, 1)
                silu(f + 1)
                act_split(f + 1, 1, 16 * c)

            ffn(0, True, True)
            with act.Fori(1, CHUNKS - 1) as c:
                ffn(c, False, True)
            ffn(CHUNKS - 1, False, False)
            for i in range(TILES):
                act.wait_ge(d_added, 16 * (CHUNKS - 1) + 2 * (i + 1))
                if i == 0:
                    act.wait_ge(hlo_ready, TILES)
                if i >= 2:
                    act.wait_ge(o_stored[i % 2], 16 * (i // 2))
                act.activation(ost[:, i % 2, :], mix[:, i, :, :].rearrange("p k t -> p (k t)"), ACT.Square,
                               accum_out=sumsq[:, 2 * TILES + 1 + i:2 * TILES + 2 + i]).then_inc(o_sumsq, 1)

        @block.vector
        def _(dve):
            dve.sem_inc(conv_step, 1)
            dve.wait_ge(consts, 6)

            def norm_x(t):
                r = META if t == 0 else P
                if t == 0:
                    dve.wait_ge(g1_loaded, 16)
                dve.wait_ge(x_rstd, t + 1)
                dve.scalar_tensor_tensor(out=xnorm[0:r, t % 2, :], in0=xin[0:r, t % 2, :], scalar=rstd[0:r, t:t + 1],
                                         in1=g1b[0:r, :], op0=ALU.mult, op1=ALU.mult).then_inc(xn_ready, 1)

            def lo_x(t):
                n, c0 = (META, 0) if t == 0 else (P, META + (t - 1) * P)
                b = (TB, Z)[t % 2]
                dve.wait_ge(xhi_ready, t + 1)
                dve.tensor_tensor(hn_lo[:, :, c0:c0 + n],
                                  ps[:, b:b + 2, :].rearrange("p b (k n) -> p (b k) n", k=4)[:, :, 0:n],
                                  hn_hi[:, :, c0:c0 + n].bitcast(F32), ALU.subtract).then_inc(xlo_ready, 1)

            norm_x(0)
            norm_x(1)
            for t in range(TILES + 1):
                lo_x(t)
                if t + 2 <= TILES:
                    norm_x(t + 2)

            def glu(g, p):
                c0, n = ALL_TOKENS[g]
                dve.wait_ge(pj_ready, pj_count("ca", g, p))
                dve.wait_ge(pj_free_act, 3 + 3 * p + 3)
                dve.tensor_tensor(u_next[:, c0:c0 + n], ps[:, pj_bank("ca", g), 0:n], u_next[:, c0:c0 + n],
                                  ALU.mult).then_inc(pj_free_dve, 1)

            def split_lo(kind, g, p):
                c0, n = tok(kind, g)
                order = DVE_G[kind, g]
                for h in range(2):
                    dve.wait_ge(pj_hi, 10 * p + 2 * order + h + 1)
                    src = ps[DH * h:DH * h + DH, pj_bank(kind, g), 0:n]
                    if kind == "k":
                        dst, high = kd[0:DH, h, 1, c0:c0 + n], kd[0:DH, h, 0, c0:c0 + n]
                    else:
                        dst, high = qst[DH:2 * DH, h, g * BANK:(g + 1) * BANK], qst[0:DH, h, g * BANK:(g + 1) * BANK]
                    last = dve.tensor_tensor(dst, src, high.bitcast(F32), ALU.subtract)
                last.then_inc(pj_free_dve, 1)

            def tap(p, j):
                base = (CONV_K + 1) * p
                if j == 0:
                    dve.wait_ge(u_ready, 2 * p + 2)
                    dve.tensor_scalar(acc[:, 0, :], u_pad[:, 0:L], parp[:, 0:1], parp[:, CONV_K:CONV_K + 1],
                                      ALU.mult, ALU.add).then_inc(conv_step, 1)
                elif j == 1:
                    dve.tensor_scalar(acc[:, 1, :], u_pad[:, 1:1 + L], parp[:, 1:2], None, ALU.mult).then_inc(conv_step, 1)
                elif j < CONV_K:
                    dve.wait_ge(conv_step, past(base + j - 1))
                    dve.scalar_tensor_tensor(out=acc[:, j % 2, :], in0=u_pad[:, j:j + L], scalar=parp[:, j:j + 1],
                                             in1=acc[:, j % 2, :], op0=ALU.mult, op1=ALU.add).then_inc(conv_step, 1)
                else:
                    dve.wait_ge(conv_step, past(base + CONV_K))
                    dve.tensor_tensor(mix[:, :, bass.ds(4 + p, 1), :].rearrange("p i a t -> p i (a t)"),
                                      acc[:, 0, :].rearrange("p (i t) -> p i t", i=TILES),
                                      acc[:, 1, :].rearrange("p (i t) -> p i t", i=TILES), ALU.add).then_inc(conv_step, 1)

            def some_taps(p, taps, n):
                for _ in range(n):
                    if taps:
                        tap(p, taps.pop(0))

            dve.wait_ge(par_t, 1)
            dve.tensor_copy(par[:, :, :], ps[:, PJ, 0:4 * NP].rearrange("p (c n) -> p c n", c=4)).then_inc(par_ready, 1)
            for g in range(3):
                glu(g, -1)
            for j in range(EARLY):
                tap(0, j)

            def mix_lo(i, part):
                dve.wait_ge(ms_hi_s, ms_count(i, part))
                dve.tensor_tensor(ms_lo[:, part, :, :], mix[:, i, 4 * part:4 * part + 4, :],
                                  ms_hi[:, part, :, :].bitcast(F32), ALU.subtract).then_inc(ms_lo_s, 1)

            def pair(p, more):
                def evac(kind, g):
                    if kind in "kq":
                        split_lo(kind, g, p)
                    elif kind == "ca":
                        glu(g, p)

                rest = list(range(EARLY, CONV_K + 1))
                groups = GROUPS if more else GROUPS[:FIRST]
                for n, (kind, g) in enumerate(groups[:-1]):
                    some_taps(p, rest, ((1, 3, 2, 3, 2, 3, 2, 3, 2, 3) if more else (1, 3, 3, 1))[n])
                    evac(kind, g)
                early = list(range(EARLY))
                for n, (h, i) in enumerate(UNITS):
                    w = width(i)
                    dve.wait_ge(z_free, past(NZ * p + CZ[n + 1]))
                    dve.tensor_tensor_scan(out=gq[:, n % 3, 0:w][:, ::-1],
                                           data0=gq[:, n % 3, 0:w][:, ::-1], data1=ones_row(w),
                                           initial=1.0, op0=ALU.mult, op1=ALU.mult).then_inc(scanned, 1)
                    dve.wait_ge(scanned, NU * p + n + 1)
                    dve.tensor_tensor(wbeta[:, n % 3, 0:w - 1], wbeta[:, n % 3, 0:w - 1], gq[:, n % 3, 1:w],
                                      ALU.mult).then_inc(w_ready, 1)
                    if n < 2 and not more:
                        some_taps(p, rest, 2 + n)
                    if n == 1:
                        evac(*groups[-1])
                    elif more and n > 7:
                        some_taps(p + 1, early, 1)
                    elif not more:
                        some_taps(p, rest, 1)
                    if not more and n == NU - 2:
                        mix_lo(0, 0)
                assert not rest and (not more or not early)

            def ones_row(w):
                return ones[:, 0:1].broadcast_to([P, w])

            with dve.Fori(0, PAIRS - 1) as p:
                pair(p, True)
            pair(PAIRS - 1, False)

            def ln_stats(i):
                dve.wait_ge(ln_t, i + 1)
                dve.bn_stats(bn6[:, :], ps[:, Z, :]).then_inc(ln_stat, 1)
                dve.wait_ge(ln_stat, i + 1)
                dve.bn_aggr(bn2[:, 2 * i:2 * i + 2], bn6[:, :]).then_inc(ln_agg, 1)

            def ln_normalise(i):
                dve.wait_ge(ln_rstd_s, i + 1)
                dve.wait_ge(ln_agg, i + 1)
                dve.tensor_scalar(mix[:, i, 4:8, :].rearrange("p k t -> p (k t)"), ps[:, Z, :],
                                  bn2[:, 2 * i:2 * i + 1], ln_rstd[:, i:i + 1], ALU.subtract, ALU.mult).then_inc(ln_norm, 1)

            def residual(i):
                dve.wait_ge(xres_loaded[i % 2], 16 * (i // 2 + 1))
                hrow = mix[:, i, :, :].rearrange("p k t -> p (k t)")
                for dh in range(2):
                    dve.wait_ge(wo_ready, 2 * i + dh + 1)
                    c = slice(dh * BANK, (dh + 1) * BANK)
                    dve.tensor_tensor(hrow[:, c], ps[:, (PJ, PV)[i % 2] + dh, :], hrow[:, c], ALU.add).then_inc(h_ready, 1)

            def norm_h(i):
                if i == 0:
                    dve.wait_ge(g2_loaded, 16)
                dve.wait_ge(h_rstd, i + 1)
                n = TILES + 1 + i
                dve.scalar_tensor_tensor(out=xn2[:, :], in0=mix[:, i, :, :].rearrange("p k t -> p (k t)"),
                                         scalar=rstd[:, n:n + 1], in1=g2b[:, :], op0=ALU.mult, op1=ALU.mult).then_inc(hn_ready, 1)

            def lo_h(i):
                dve.wait_ge(hhi_ready, i + 1)
                dve.tensor_tensor(hn2_lo[:, :, i * P:(i + 1) * P],
                                  ps[:, TB:TB + 2, :].rearrange("p b (k t) -> p (b k) t", k=4),
                                  hn2_hi[:, :, i * P:(i + 1) * P].bitcast(F32), ALU.subtract).then_inc(hlo_ready, 1)

            ln_stats(0)
            ln_normalise(0)
            mix_lo(1, 0)
            for i in range(TILES):
                if i >= 1:
                    residual(i - 1)
                if i >= 2:
                    lo_h(i - 2)
                if i + 1 < TILES:
                    ln_stats(i + 1)
                    ln_normalise(i + 1)
                mix_lo(i, 1)
                if i >= 1:
                    norm_h(i - 1)
                if i + 2 < TILES:
                    mix_lo(i + 2, 0)
            residual(TILES - 1)
            lo_h(TILES - 2)
            norm_h(TILES - 1)
            lo_h(TILES - 1)

            def products(f):
                for tg in range(2):
                    c = slice(tg * BANK, (tg + 1) * BANK)
                    dve.wait_ge(silu_done, 2 * f + tg + 1)
                    dve.wait_ge(u_ready2, 2 * f + tg + 1)
                    dve.wait_ge(act_lo_s, f)
                    dve.tensor_tensor(prod[:, c], sil[:, c], ps[:, Z + tg, :], ALU.mult).then_inc(prod_done, 1)

            def act_low(f, slot):
                dve.wait_ge(act_hi_s, f + 1)
                dve.tensor_tensor(act_lo[:, slot, :], prod[:, :], act_hi[:, slot, :].bitcast(F32),
                                  ALU.subtract).then_inc(act_lo_s, 1)

            def down(c):
                for i in range(TILES):
                    for dh in range(2):
                        n = 2 * i + dh
                        s = slice(dh * BANK, (dh + 1) * BANK)
                        hrow = mix[:, i, :, :].rearrange("p k t -> p (k t)")[:, s]
                        dve.wait_ge(d_ready, 16 * c + n + 1)
                        dve.wait_ge(d_added, 16 * c)
                        dve.tensor_tensor(hrow, ps[:, TB + n % 4, :], hrow, ALU.add).then_inc(d_added, 1)

            def ffn(c, first):
                f = 2 * c
                products(f)
                if not first:
                    down(c - 1)
                act_low(f, 0)
                products(f + 1)
                act_low(f + 1, 1)

            ffn(0, True)
            with dve.Fori(1, CHUNKS) as c:
                ffn(c, False)
            def norm_out(i):
                if i == 0:
                    dve.wait_ge(gf_loaded, 16)
                dve.wait_ge(o_rstd, i + 1)
                n = 2 * TILES + 1 + i
                dve.scalar_tensor_tensor(out=ost[:, i % 2, :], in0=mix[:, i, :, :].rearrange("p k t -> p (k t)"),
                                         scalar=rstd[:, n:n + 1], in1=gfb[:, :], op0=ALU.mult, op1=ALU.mult).then_inc(o_ready, 1)

            c = CHUNKS - 1
            for i in range(TILES):
                for dh in range(2):
                    n = 2 * i + dh
                    s = slice(dh * BANK, (dh + 1) * BANK)
                    hrow = mix[:, i, :, :].rearrange("p k t -> p (k t)")[:, s]
                    dve.wait_ge(d_ready, 16 * c + n + 1)
                    dve.wait_ge(d_added, 16 * c)
                    dve.tensor_tensor(hrow, ps[:, TB + n % 4, :], hrow, ALU.add).then_inc(d_added, 1)
                if i:
                    norm_out(i - 1)
            norm_out(TILES - 1)

        @block.tensor
        def _(pe):
            for s in (z_ready, t_ready, pv_used):
                pe.sem_inc(s, 1)
            pe.wait_ge(consts, 9)

            def transpose_x(t):
                r = META if t == 0 else P
                b = (TB, Z)[t % 2]
                pe.wait_ge(xn_ready, t + 1)
                if t >= 2:
                    pe.wait_ge(xlo_ready, t - 1)
                for k in range(KD):
                    last = pe.transpose(ps[:, b + k // 4, (k % 4) * P:(k % 4) * P + r],
                                        xnorm[0:r, t % 2, k * P:(k + 1) * P], ident[0:r, 0:r])
                last.then_inc(xt_ready, 1)

            def project_v(b):
                c0 = min(b * P, T - P)
                pe.wait_ge(xlo_ready, min(b + 2, TILES + 1))
                if b >= 2:
                    pe.wait_ge(v_copied, b - 1)
                hn, wv = (hn_hi, hn_lo), (wv_hi, wv_lo)
                for k in range(KD):
                    if b == 0 and k % 2 == 0:
                        pe.wait_ge(wlo_done, CH_V + k // 2 + 1)
                    for s, m in PASSES:
                        last = pe.matmul(ps[:, PV + b % 2, :], hn[s][:, k, c0:c0 + P], wv[m][:, k, :],
                                         start=(k == 0 and s == m == 0), stop=(k == KD - 1 and s == 1))
                last.then_inc(v_ready, 1)

            for t in range(TILES + 1):
                transpose_x(t)
                if t >= 2 and t < TILES:
                    project_v(t - 2)
            pe.wait_ge(par_loaded, 64)
            for c in range(4):
                last = pe.transpose(ps[:, PJ, c * NP:(c + 1) * NP], par_nat[:, c * P:(c + 1) * P], ident[0:NP, 0:NP])
            last.then_inc(par_t, 1)

            def groups(p, which, loop):
                for kind, g in which:
                    idx = GROUPS.index((kind, g))
                    waits = []
                    if g == 0:
                        if not loop:
                            n = {"cg": CH_CG0, "ca": CH_CA0}[kind]
                        else:
                            n = {"k": CH_K0 + 4 * p, "q": CH_Q0 + 4 * p, "cg": CH_LOOP + 4 * p, "ca": CH_LOOP + 1 + 4 * p}[kind]
                        waits.append((wlo_done, n + 1))
                    if idx >= 2:
                        before = GROUPS[idx - 2]
                        if loop or idx - 2 >= FIRST:
                            waits.append(freed(*before, p))
                    else:
                        waits.append(freed(*GROUPS[9 + (idx + 1) % 2], p - 1))
                    if loop and idx == 1:
                        waits.append((z_free, past(NZ * p)))
                    if not loop and idx == FIRST:
                        waits.append((par_ready, 1))
                        waits.append((xlo_ready, TILES + 1))
                    slot = 0 if kind in ("k", "cg") else 1
                    c0, n = tok(kind, g)
                    for w in waits:
                        pe.wait_ge(*w)
                    w_, hn = (wp_hi, wp_lo), (hn_hi, hn_lo)
                    for k in range(KD):
                        for s, m in PASSES:
                            last = pe.matmul(ps[:, pj_bank(kind, g), 0:n], w_[s][:, slot, k, :], hn[m][:, k, c0:c0 + n],
                                             start=(k == 0 and s == m == 0), stop=(k == KD - 1 and s == 1))
                    last.then_inc(pj_ready, 1)

            groups(-1, GROUPS[FIRST:], False)
            for b in range(TILES - 2, TILES + 1):
                project_v(b)

            def pair(p, more, before_last):
                todo = GROUPS if more else GROUPS[:FIRST]
                groups(p, todo[1:-1], True)

                def scores(n):
                    h, i = UNITS[n]
                    if n == 0:
                        pe.wait_ge(k_dup, 16 * (p + 1))
                    if n == 0 or i >= 4 and all(j < 4 for _, j in UNITS[:n]):
                        pe.wait_ge(pj_free_dve, 3 + 8 * p + 4 + i // 4)
                    d0 = META + i * P
                    for c, (c0, cols, used) in enumerate(z_chunks(i)):
                        m = CZ[n] + c
                        if z_before(m):
                            pe.wait_ge(z_free, past(NZ * p + z_before(m)))
                        if m in (2, 3):
                            pe.wait_ge(*freed(*(todo[-2] if m == 2 else todo[-1]), p))
                        for part in range(2):
                            last = pe.matmul(ps[:, Z_BANKS[m], 0:cols], qst[:, h, i * P:(i + 1) * P],
                                             kd[:, h, part, c0:c0 + cols], start=(part == 0),
                                             stop=(part == 1 and c0 + used <= d0))
                        lo, hi = max(d0, c0), c0 + used
                        if hi > lo:
                            last = pe.matmul(ps[:, Z_BANKS[m], lo - c0:hi - c0], ident_bf[:, :],
                                             mask_bf[:, lo - d0:hi - d0], start=False, stop=True)
                        last.then_inc(z_ready, 1)

                def transpose_w(n, banks):
                    h, i = UNITS[n]
                    for b in banks:
                        m = CT[n] + b
                        if b == 0:
                            pe.wait_ge(w_ready, NU * p + n + 1)
                            pe.wait_ge(tail_zeroed, NU * p + n + 1)
                        pe.wait_ge(t_copied, past(NT * p + max(m - 1, 0)))
                        for j, kb in enumerate(t_banks(i)[b]):
                            last = pe.transpose(ps[:, TB + m % 2, j * P:(j + 1) * P],
                                                wbeta[:, n % 3, kb * P:(kb + 1) * P], ident[:, :])
                        last.then_inc(t_ready, 1)

                def attend(n):
                    h, i = UNITS[n]
                    if n == 0:
                        pe.wait_ge(pv_evac, past(NG * p))
                        pe.wait_ge(v_loaded, 32 * (p + 1))
                    for b, blocks in enumerate(t_banks(i)):
                        m = CT[n] + b
                        pe.wait_ge(t_copied, past(NT * p + m + 1))
                        for j, kb in enumerate(blocks):
                            last = pe.matmul(ps[DH * h:DH * h + DH, PV + i // 4, (i % 4) * P:(i % 4 + 1) * P],
                                             vs[:, kb, DH * h:DH * h + DH], w_t[:, m % 4, j, :],
                                             start=(kb == 0), stop=(kb == i + 1))
                        last.then_inc(pv_used, 1)

                for n in range(HELD_BACK):
                    scores(n)
                groups(p, todo[-1:], True)
                for n in range(NU + 1):
                    if n + 2 < NU:
                        scores(n + 2)
                    if n < NU:
                        nb = len(t_banks(UNITS[n][1]))
                        transpose_w(n, range(min(2, nb)))
                    if n == NU:
                        before_last()
                    if n:
                        attend(n - 1)
                    if n < NU:
                        transpose_w(n, range(2, nb))

            def next_k(p):
                pe.wait_ge(z_free, past(NZ * p + max(m + 1 for m in range(NZ) if Z_BANKS[m] == PJ)))
                groups(p + 1, GROUPS[:1], True)

            groups(0, GROUPS[:1], True)
            with pe.Fori(0, PAIRS - 1) as p:
                pair(p, True, lambda: next_k(p))

            def ln_forward(i):
                if i == 0:
                    pe.wait_ge(conv_step, past((CONV_K + 1) * PAIRS))
                else:
                    pe.wait_ge(ln_norm, i)
                for c in range(4):
                    last = pe.transpose(ps[:, Z, c * P:(c + 1) * P], mix[:, i, 4 + c, :], ident[:, :])
                last.then_inc(ln_t, 1)

            def ln_backward(i):
                pe.wait_ge(ln_norm, i + 1)
                pe.wait_ge(ln_silu, 4 * i)
                for c in range(4):
                    last = pe.transpose(ps[:, Z + 1, c * P:(c + 1) * P], mix[:, i, 4 + c, :], ident[:, :])
                last.then_inc(ln_back, 1)

            def w_out_part(i, part):
                if i == 0:
                    pe.wait_ge(wo_lo_s, 4 * (part + 1))
                pe.wait_ge(ms_lo_s, ms_count(i, part))
                ms, wo = (ms_hi, ms_lo), (wo_hi, wo_lo)
                for dh in range(2):
                    if i >= 2 and part == 0:
                        pe.wait_ge(h_ready, 2 * (i - 2) + dh + 1)
                    for k in range(4):
                        for s, m in PASSES:
                            last = pe.matmul(ps[:, (PJ, PV)[i % 2] + dh, :], ms[s][:, part, k, :],
                                             wo[m][:, 4 * part + k, dh * BANK:(dh + 1) * BANK],
                                             start=(part == 0 and k == 0 and s == m == 0),
                                             stop=(part == 1 and k == 3 and s == 1))
                    if part:
                        last.then_inc(wo_ready, 1)
                if not part:
                    last.then_inc(ms_used, 1)

            def transpose_h(i):
                pe.wait_ge(hn_ready, i + 1)
                pe.wait_ge(hlo_ready, i)
                for k in range(KD):
                    last = pe.transpose(ps[:, TB + k // 4, (k % 4) * P:(k % 4 + 1) * P],
                                        xn2[:, k * P:(k + 1) * P], ident[:, :])
                last.then_inc(ht_ready, 1)

            def first_tile():
                pe.wait_ge(z_free, past(NZ * PAIRS))
                ln_forward(0)
                w_out_part(0, 0)
                ln_backward(0)

            pair(PAIRS - 1, False, first_tile)
            pe.wait_ge(pv_evac, past(NG * PAIRS))
            for i in range(TILES):
                if i + 1 < TILES:
                    ln_forward(i + 1)
                    w_out_part(i + 1, 0)
                w_out_part(i, 1)
                if i >= 1:
                    transpose_h(i - 1)
                if i + 1 < TILES:
                    ln_backward(i + 1)

            def gate_up(f, slot, before_second=None):
                hn2 = (hn2_hi, hn2_lo)
                pe.wait_ge(wlo_done, CH_GU + 2 * f + 2)
                for tg in range(2):
                    if tg and before_second:
                        before_second()
                    for n, (bank, s_, free) in enumerate(((PJ + tg, g_ready, silu_done), (Z + tg, u_ready2, prod_done))):
                        pe.wait_ge(free, 2 * f)
                        w_ = (gu_hi[slot], gu_lo[slot])
                        for k in range(KD):
                            for s, m in PASSES:
                                last = pe.matmul(ps[:, bank, :], w_[s][:, n, k, :],
                                                 hn2[m][:, k, tg * BANK:(tg + 1) * BANK],
                                                 start=(k == 0 and s == m == 0), stop=(k == KD - 1 and s == 1))
                        last.then_inc(s_, 1)

            def down(c, first):
                pe.wait_ge(act_lo_s, 2 * c + 2)
                pe.wait_ge(dlo_done, past(c + 1))
                a, w_ = (act_hi, act_lo), (wd_hi, wd_lo)
                for i in range(TILES):
                    for dh in range(2):
                        n = 2 * i + dh
                        if not (first and n < 4):
                            pe.wait_ge(d_added, 16 * c + n - 3)
                        for t in range(2):
                            for s, m in PASSES:
                                last = pe.matmul(ps[:, TB + n % 4, :], a[s][:, t, i * P:(i + 1) * P],
                                                 w_[m][:, t, dh * BANK:(dh + 1) * BANK],
                                                 start=(t == 0 and s == m == 0), stop=(t == 1 and s == 1))
                        last.then_inc(d_ready, 1)

            def last_tile():
                transpose_h(TILES - 1)
                pe.wait_ge(hlo_ready, TILES)

            pe.wait_ge(hlo_ready, TILES // 2)
            gate_up(0, 0, last_tile)
            gate_up(1, 1)
            gate_up(2, 0)
            down(0, True)
            gate_up(3, 1)
            with pe.Fori(2, CHUNKS) as c:
                gate_up(2 * c, 0)
                down(c - 1, False)
                gate_up(2 * c + 1, 1)
            down(CHUNKS - 1, False)


_INS = ["x", "meta_tokens", "mix_norm_g", "w_in", "conv_dw_w", "conv_dw_b", "conv_ln_g", "conv_ln_b", "w_out",
        "ffn_norm_g", "w_gate", "w_up", "w_down", "final_norm_g"]


def kernel(**inputs):
    import numpy as np
    import concourse.bacc as bacc
    from concourse.bass_utils import run_bass_kernel_spmd

    nc = bacc.Bacc("TRN2", target_bir_lowering=False, num_devices=1)
    arrays, args = {}, []
    for name in _INS:
        a = np.ascontiguousarray(inputs[name])
        arrays[f"in_{name}"] = a
        args.append(nc.dram_tensor(f"in_{name}", a.shape, mybir.dt.from_np(a.dtype), kind="ExternalInput").ap())
    x = inputs["x"]
    out = nc.dram_tensor("out", x.shape, F32, kind="ExternalOutput").ap()
    tokens = x.shape[1] + inputs["meta_tokens"].shape[0]
    width = inputs["w_out"].shape[1] - inputs["conv_dw_w"].shape[2]
    v_dram = nc.dram_tensor("v_dram", (tokens, width), F32).ap()
    hybrid_block(nc, *args, out, v_dram)
    r = run_bass_kernel_spmd(nc, [arrays], core_ids=[0])
    return r.results[0]["out"]
```
